# Optimizing a Trainium2 kernel written in Bass

```python
import math
import jax, jax.numpy as jnp
from jax import lax
import numpy as np
import jax
import jax.numpy as jnp

D_MODEL = 1024
BATCH = 1
SEQ = 256
DEPTH = 2

CHUNK = 64
N_MEM = 256
D_MIX = D_MODEL
D_GLA = D_MIX // 2
D_SGU = D_MIX - D_GLA
GLA_HEADS = 4
D_QK = D_GLA // 2
GLA_DK = D_QK // GLA_HEADS
GLA_DV = D_GLA // GLA_HEADS
GATE_RANK = 16
GATE_TEMP = 16.0
SGU_GROUPS = 4
SGU_BLOCK = 128
SGU_CH = D_SGU // SGU_GROUPS
XATTN_HEADS = 4
XATTN_DH = D_MODEL // XATTN_HEADS
N_EXPERTS = 16
N_EXPERT_GROUPS = 4
EXPERTS_PER_GROUP = N_EXPERTS // N_EXPERT_GROUPS
TOP_K = 2
D_EXPERT = D_MODEL // 2
DN_ALPHA = (2.0 * DEPTH) ** 0.25
DN_BETA = (8.0 * DEPTH) ** -0.25
LN_EPS = 1e-5
RMS_EPS = 1e-6
D_IN = 2 * D_QK + 2 * D_GLA + GATE_RANK + 2 * D_SGU


def layer_norm(x, g, b):
    xf = x.astype(jnp.float32)
    mu = jnp.mean(xf, axis=-1, keepdims=True)
    var = jnp.mean(jnp.square(xf - mu), axis=-1, keepdims=True)
    y = (xf - mu) * lax.rsqrt(var + LN_EPS)
    return (y * g.astype(jnp.float32) + b.astype(jnp.float32)).astype(x.dtype)

def split_proj(p):
    sizes = (D_QK, D_QK, D_GLA, D_GLA, GATE_RANK, D_SGU, D_SGU)
    outs, start = [], 0
    for s in sizes:
        outs.append(p[..., start:start + s])
        start += s
    return outs

def gla_group(q, k, v, r, a_low, w_a2, b_a, gn_g):
    B, S, _ = q.shape
    nc = S // CHUNK
    log_a = jax.nn.log_sigmoid((a_low @ w_a2 + b_a).astype(jnp.float32)) / GATE_TEMP

    def to_chunks(t, d):
        return t.astype(jnp.float32).reshape(B, nc, CHUNK, GLA_HEADS, d).transpose(1, 0, 3, 2, 4)

    qc = to_chunks(q, GLA_DK) * (GLA_DK ** -0.5)
    kc = to_chunks(k, GLA_DK)
    vc = to_chunks(v, GLA_DV)
    gc = to_chunks(log_a, GLA_DK)

    def step(state, inp):
        q_c, k_c, v_c, g_c = inp
        bcum = jnp.cumsum(g_c, axis=2)
        b_last = bcum[:, :, -1:, :]
        k_dec = k_c * jnp.exp(b_last - bcum)
        state = jnp.exp(b_last[:, :, 0, :])[..., None] * state + jnp.einsum('bhck,bhcv->bhkv', k_dec, v_c)
        o = jnp.einsum('bhck,bhkv->bhcv', q_c, state)
        return state, o

    s0 = jnp.zeros((B, GLA_HEADS, GLA_DK, GLA_DV), jnp.float32)
    _, o = lax.scan(step, s0, (qc, kc, vc, gc))
    o = o.transpose(1, 0, 3, 2, 4).reshape(B, S, GLA_HEADS, GLA_DV)
    o = o * lax.rsqrt(jnp.mean(jnp.square(o), axis=-1, keepdims=True) + RMS_EPS)
    o = o.reshape(B, S, D_GLA) * gn_g.astype(jnp.float32)
    out = o * jax.nn.silu(r.astype(jnp.float32))
    return out.astype(q.dtype)

def sgu_group(u, v, w_s, b_s, ln_g, ln_b):
    B, S, _ = u.shape
    nb = S // SGU_BLOCK
    u = jax.nn.gelu(u)
    v = jax.nn.gelu(v).reshape(B, S, SGU_GROUPS, SGU_CH)
    v = layer_norm(v, ln_g.reshape(SGU_GROUPS, SGU_CH), ln_b.reshape(SGU_GROUPS, SGU_CH))
    v = v.reshape(B, nb, SGU_BLOCK, SGU_GROUPS, SGU_CH)
    pos = jnp.arange(SGU_BLOCK)
    mask = (pos[None, :] // CHUNK) <= (pos[:, None] // CHUNK)
    w_m = jnp.where(mask[None], w_s, jnp.zeros_like(w_s))
    mixed = jnp.einsum('gts,bnsgc->bntgc', w_m, v) + b_s.T[None, None, :, :, None]
    out = u.reshape(B, nb, SGU_BLOCK, SGU_GROUPS, SGU_CH) * mixed
    return out.reshape(B, S, D_SGU)

def mem_xattn(x, mem, wq, wk, wv, wo):
    B, S, _ = x.shape
    M = mem.shape[1]
    q = (x @ wq).reshape(B, S, XATTN_HEADS, XATTN_DH)
    k = (mem @ wk).reshape(B, M, XATTN_HEADS, XATTN_DH)
    v = (mem @ wv).reshape(B, M, XATTN_HEADS, XATTN_DH)
    s = jnp.einsum('bshd,bmhd->bhsm', q, k).astype(jnp.float32) * (XATTN_DH ** -0.5)
    p = jax.nn.softmax(s, axis=-1).astype(v.dtype)
    o = jnp.einsum('bhsm,bmhd->bshd', p, v).reshape(B, S, D_MODEL)
    return o @ wo

def grouped_moe(x, w_router, b_router, w_gate, w_up, w_down):
    B, S, D = x.shape
    xt = x.reshape(B * S, D)
    scores = jax.nn.softmax((xt @ w_router + b_router).astype(jnp.float32), axis=-1)
    grp = scores.reshape(-1, N_EXPERT_GROUPS, EXPERTS_PER_GROUP)
    group_score = jnp.sum(lax.top_k(grp, TOP_K)[0], axis=-1)
    g_sel = jnp.argmax(group_score, axis=-1)
    in_grp = jnp.sum(grp * jax.nn.one_hot(g_sel, N_EXPERT_GROUPS, dtype=jnp.float32)[:, :, None], axis=1)
    top_w, top_i = lax.top_k(in_grp, TOP_K)
    top_w = top_w / jnp.sum(top_w, axis=-1, keepdims=True)
    eid = g_sel[:, None] * EXPERTS_PER_GROUP + top_i
    gate = jnp.sum(jax.nn.one_hot(eid, N_EXPERTS, dtype=jnp.float32) * top_w[..., None], axis=1)
    gate = gate.astype(x.dtype)
    y = jnp.zeros_like(xt)
    for e in range(N_EXPERTS):
        h = jax.nn.silu(xt @ w_gate[e]) * (xt @ w_up[e])
        y = y + gate[:, e:e + 1] * (h @ w_down[e])
    return y.reshape(B, S, D)

def first_inputs(seed: int = 0) -> dict:
    key = jax.random.key(seed)
    ks = jax.random.split(key, 24)
    f32 = jnp.float32

    def nrm(k, shape, fan_in, scale=1.0):
        return jax.random.normal(k, shape, f32) * (scale * fan_in ** -0.5)

    def gain(k, shape):
        return 1.0 + 0.02 * jax.random.normal(k, shape, f32)

    return {
        "x": jax.random.normal(ks[0], (BATCH, SEQ, D_MODEL), f32),
        "mem": jax.random.normal(ks[1], (BATCH, N_MEM, D_MODEL), f32),
        "w_in": nrm(ks[2], (DEPTH, D_MODEL, D_IN), D_MODEL),
        "w_a2": nrm(ks[3], (DEPTH, GATE_RANK, D_QK), GATE_RANK),
        "b_a": 1.0 + 0.5 * jax.random.normal(ks[4], (DEPTH, D_QK), f32),
        "gla_norm_g": gain(ks[5], (DEPTH, D_GLA)),
        "w_s": nrm(ks[6], (DEPTH, SGU_GROUPS, SGU_BLOCK, SGU_BLOCK), SGU_BLOCK),
        "b_s": gain(ks[7], (DEPTH, SGU_GROUPS, SGU_BLOCK)),
        "sgu_ln_g": gain(ks[8], (DEPTH, D_SGU)),
        "sgu_ln_b": 0.02 * jax.random.normal(ks[9], (DEPTH, D_SGU), f32),
        "w_out": nrm(ks[10], (DEPTH, D_MIX, D_MODEL), D_MIX, DN_BETA),
        "wq_x": nrm(ks[11], (DEPTH, D_MODEL, D_MODEL), D_MODEL),
        "wk_x": nrm(ks[12], (DEPTH, D_MODEL, D_MODEL), D_MODEL),
        "wv_x": nrm(ks[13], (DEPTH, D_MODEL, D_MODEL), D_MODEL),
        "wo_x": nrm(ks[14], (DEPTH, D_MODEL, D_MODEL), D_MODEL, DN_BETA),
        "w_router": nrm(ks[15], (D_MODEL, N_EXPERTS), D_MODEL),
        "b_router": 0.01 * jax.random.normal(ks[16], (N_EXPERTS,), f32),
        "w_gate": nrm(ks[17], (DEPTH, N_EXPERTS, D_MODEL, D_EXPERT), D_MODEL),
        "w_up": nrm(ks[18], (DEPTH, N_EXPERTS, D_MODEL, D_EXPERT), D_MODEL),
        "w_down": nrm(ks[19], (DEPTH, N_EXPERTS, D_EXPERT, D_MODEL), D_EXPERT, DN_BETA),
        "ln_g": gain(ks[20], (DEPTH, 3, D_MODEL)),
        "ln_b": 0.02 * jax.random.normal(ks[21], (DEPTH, 3, D_MODEL), f32),
    }

def first_block(x, mem, w_in, w_a2, b_a, gla_norm_g, w_s, b_s, sgu_ln_g, sgu_ln_b, w_out,
              wq_x, wk_x, wv_x, wo_x, w_router, b_router, w_gate, w_up, w_down, ln_g, ln_b):
    for l in range(DEPTH):
        q, k, v, r, a_low, u, v_sgu = split_proj(x @ w_in[l])
        y_gla = gla_group(q, k, v, r, a_low, w_a2[l], b_a[l], gla_norm_g[l])
        y_sgu = sgu_group(u, v_sgu, w_s[l], b_s[l], sgu_ln_g[l], sgu_ln_b[l])
        h = jnp.concatenate([y_gla, y_sgu], axis=-1) @ w_out[l]
        x = layer_norm(DN_ALPHA * x + h, ln_g[l, 0], ln_b[l, 0])
        h = mem_xattn(x, mem, wq_x[l], wk_x[l], wv_x[l], wo_x[l])
        x = layer_norm(DN_ALPHA * x + h, ln_g[l, 1], ln_b[l, 1])
        h = grouped_moe(x, w_router, b_router, w_gate[l], w_up[l], w_down[l])
        x = layer_norm(DN_ALPHA * x + h, ln_g[l, 2], ln_b[l, 2])
    return x


DEPTH_2 = 1

F32 = jnp.float32
EPS = 1e-6
PLE_DIM = 256

A_HEADS = 8
A_HEAD_DIM = 64
A_WIDTH = A_HEADS * A_HEAD_DIM
MOBA_BLOCK = 256
MOBA_TOPK = 3
MOBA_QCHUNK = 16

SSD_D_INNER = D_MODEL
SSD_HEAD_DIM = 64
SSD_HEADS = SSD_D_INNER // SSD_HEAD_DIM
SSD_GROUPS = 2
SSD_D_STATE = 128
SSD_CONV = 4
SSD_CHUNK = 256
SSD_CONV_DIM = SSD_D_INNER + 2 * SSD_GROUPS * SSD_D_STATE

MOE_GROUPS = 4
MOE_EXPERTS_PER_GROUP = 4
MOE_EXPERTS = MOE_GROUPS * MOE_EXPERTS_PER_GROUP
MOE_TOPK = 2
MOE_D_FF = 512

OFF_Q = 0
OFF_K = OFF_Q + A_WIDTH
OFF_V = OFF_K + A_WIDTH
OFF_Z = OFF_V + A_WIDTH
OFF_XBC = OFF_Z + SSD_D_INNER
OFF_DT = OFF_XBC + SSD_CONV_DIM
OFF_GA = OFF_DT + SSD_HEADS
OFF_GB = OFF_GA + D_MODEL
IN_DIM = OFF_GB + D_MODEL


def rms_norm(x, g):
    xf = x.astype(F32)
    y = xf * lax.rsqrt(jnp.mean(xf * xf, axis=-1, keepdims=True) + EPS)
    return (y * g.astype(F32)).astype(x.dtype)

def alibi_slopes(n):
    return 2.0 ** (-8.0 * jnp.arange(1, n + 1, dtype=F32) / n)

def moba_attention(q, k, v):
    bsz, s, nh, hd = q.shape
    nb = -(-s // MOBA_BLOCK)
    s_pad = nb * MOBA_BLOCK
    pad = ((0, 0), (0, s_pad - s), (0, 0), (0, 0))
    q, k, v = [jnp.pad(t, pad).transpose(0, 2, 1, 3) for t in (q, k, v)]
    scale = hd ** -0.5
    kb = k.reshape(bsz, nh, nb, MOBA_BLOCK, hd)
    vb = v.reshape(bsz, nh, nb, MOBA_BLOCK, hd)
    k_mean = jnp.mean(kb.astype(F32), axis=3)
    gate = jnp.einsum('bhtd,bhnd->bhtn', q.astype(F32), k_mean)
    q_blk = jnp.arange(s_pad) // MOBA_BLOCK
    past = jnp.arange(nb)[None, :] < q_blk[:, None]
    gate = jnp.where(past[None, None], gate, -jnp.inf)
    topk = min(MOBA_TOPK, nb)
    _, top_idx = lax.top_k(gate, topk)
    sel_valid = jnp.arange(topk)[None, :] < q_blk[:, None]
    slopes = alibi_slopes(nh)[None, :, None, None]
    bi = jnp.arange(bsz)[:, None, None, None]
    hi = jnp.arange(nh)[None, :, None, None]
    offs = jnp.arange(MOBA_BLOCK)
    n_chunks = s_pad // MOBA_QCHUNK

    def chunk(c):
        t0 = c * MOBA_QCHUNK
        qc = lax.dynamic_slice_in_dim(q, t0, MOBA_QCHUNK, axis=2)
        idx = lax.dynamic_slice_in_dim(top_idx, t0, MOBA_QCHUNK, axis=2)
        valid = lax.dynamic_slice_in_dim(sel_valid, t0, MOBA_QCHUNK, axis=0)
        t = t0 + jnp.arange(MOBA_QCHUNK)
        kg = kb[bi, hi, idx]
        vg = vb[bi, hi, idx]
        s_sel = jnp.einsum('bhqd,bhqkld->bhqkl', qc, kg, preferred_element_type=F32) * scale
        kpos = idx[..., None] * MOBA_BLOCK + offs
        s_sel = s_sel - slopes[..., None] * (t[:, None, None] - kpos).astype(F32)
        s_sel = jnp.where(valid[:, :, None], s_sel, -jnp.inf)
        blk0 = (t0 // MOBA_BLOCK) * MOBA_BLOCK
        ko = lax.dynamic_slice_in_dim(k, blk0, MOBA_BLOCK, axis=2)
        vo = lax.dynamic_slice_in_dim(v, blk0, MOBA_BLOCK, axis=2)
        s_own = jnp.einsum('bhqd,bhld->bhql', qc, ko, preferred_element_type=F32) * scale
        dist = t[:, None] - (blk0 + offs)[None, :]
        s_own = jnp.where(dist >= 0, s_own - slopes * dist.astype(F32), -jnp.inf)
        sc = jnp.concatenate([s_sel.reshape(bsz, nh, MOBA_QCHUNK, topk * MOBA_BLOCK), s_own], axis=-1)
        pr = jax.nn.softmax(sc, axis=-1).astype(v.dtype)
        p_sel = pr[..., :topk * MOBA_BLOCK].reshape(bsz, nh, MOBA_QCHUNK, topk, MOBA_BLOCK)
        p_own = pr[..., topk * MOBA_BLOCK:]
        return (jnp.einsum('bhqkl,bhqkld->bhqd', p_sel, vg)
                + jnp.einsum('bhql,bhld->bhqd', p_own, vo))

    out = lax.map(chunk, jnp.arange(n_chunks))
    out = out.transpose(1, 2, 0, 3, 4).reshape(bsz, nh, s_pad, hd)[:, :, :s]
    return out.transpose(0, 2, 1, 3)

def causal_depthwise_conv(u, w, b):
    c = u.shape[-1]
    out = lax.conv_general_dilated(u, w[:, None, :].astype(u.dtype), window_strides=(1,),
                                   padding=[(SSD_CONV - 1, 0)],
                                   dimension_numbers=('NWC', 'WIO', 'NWC'),
                                   feature_group_count=c)
    return out + b

def segsum(a):
    tlen = a.shape[-1]
    cs = jnp.cumsum(a, axis=-1)
    diff = cs[..., :, None] - cs[..., None, :]
    mask = jnp.tril(jnp.ones((tlen, tlen), dtype=bool))
    return jnp.where(mask, diff, -jnp.inf)

def ssd_chunked_scan(x, dt, a, b_in, c_in):
    bsz, s, nh, hp = x.shape
    ng, ns = b_in.shape[2], b_in.shape[3]
    hpg = nh // ng
    nc = -(-s // SSD_CHUNK)
    sp = nc * SSD_CHUNK

    def padt(t):
        return jnp.pad(t.astype(F32), [(0, 0), (0, sp - s)] + [(0, 0)] * (t.ndim - 2))

    x, dt, b_in, c_in = padt(x), padt(dt), padt(b_in), padt(c_in)
    xdt = (x * dt[..., None]).reshape(bsz, nc, SSD_CHUNK, ng, hpg, hp)
    da = (dt * a.astype(F32)).reshape(bsz, nc, SSD_CHUNK, ng, hpg).transpose(0, 3, 4, 1, 2)
    bc = b_in.reshape(bsz, nc, SSD_CHUNK, ng, ns)
    cc = c_in.reshape(bsz, nc, SSD_CHUNK, ng, ns)
    da_cs = jnp.cumsum(da, axis=-1)
    decay_in = jnp.exp(segsum(da))
    cb = jnp.einsum('bclgn,bcsgn->bgcls', cc, bc)
    y_diag = jnp.einsum('bgcls,bgjcls,bcsgjp->bclgjp', cb, decay_in, xdt)
    decay_to_end = jnp.exp(da_cs[..., -1:] - da_cs)
    chunk_states = jnp.einsum('bclgn,bgjcl,bclgjp->cbgjpn', bc, decay_to_end, xdt)
    chunk_decay = jnp.exp(da_cs[..., -1]).transpose(3, 0, 1, 2)

    def carry_state(h, inp):
        st, dec = inp
        return h * dec[..., None, None] + st, h

    h0 = jnp.zeros(chunk_states.shape[1:], F32)
    _, h_in = lax.scan(carry_state, h0, (chunk_states, chunk_decay))
    y_off = jnp.einsum('bclgn,cbgjpn,bgjcl->bclgjp', cc, h_in, jnp.exp(da_cs))
    return (y_diag + y_off).reshape(bsz, sp, nh, hp)[:, :s]

def ssd_mixer(z, xbc, dt_raw, conv_w, conv_b, dt_bias, a_log, d_skip, norm_g):
    bsz, s, _ = z.shape
    xbc = jax.nn.silu(causal_depthwise_conv(xbc, conv_w, conv_b))
    xs = xbc[..., :SSD_D_INNER].reshape(bsz, s, SSD_HEADS, SSD_HEAD_DIM)
    gs = SSD_GROUPS * SSD_D_STATE
    b_in = xbc[..., SSD_D_INNER:SSD_D_INNER + gs].reshape(bsz, s, SSD_GROUPS, SSD_D_STATE)
    c_in = xbc[..., SSD_D_INNER + gs:].reshape(bsz, s, SSD_GROUPS, SSD_D_STATE)
    dt = jax.nn.softplus(dt_raw.astype(F32) + dt_bias.astype(F32))
    a = -jnp.exp(a_log.astype(F32))
    y = ssd_chunked_scan(xs, dt, a, b_in, c_in)
    y = y + d_skip.astype(F32)[:, None] * xs.astype(F32)
    u = (y.reshape(bsz, s, SSD_D_INNER) * jax.nn.silu(z.astype(F32)))
    u = u.reshape(bsz, s, SSD_GROUPS, SSD_D_INNER // SSD_GROUPS)
    u = u * lax.rsqrt(jnp.mean(u * u, axis=-1, keepdims=True) + EPS)
    return (u.reshape(bsz, s, SSD_D_INNER) * norm_g.astype(F32)).astype(z.dtype)

def hier_moe(h, w_rg, b_rg, w_re, b_re, w_gate, w_up, w_down):
    bsz, s, _ = h.shape
    hf = h.astype(F32)
    g_logits = hf @ w_rg.astype(F32) + b_rg.astype(F32)
    g_prob = jax.nn.softmax(g_logits, axis=-1)
    g_pw, g_sel = lax.top_k(g_prob, 1)
    e_logits = (hf @ w_re.astype(F32) + b_re.astype(F32)).reshape(bsz, s, MOE_GROUPS, MOE_EXPERTS_PER_GROUP)
    e_in_group = jnp.take_along_axis(e_logits, g_sel[..., None], axis=2)[:, :, 0]
    e_val, e_idx = lax.top_k(e_in_group, MOE_TOPK)
    e_w = jax.nn.softmax(e_val, axis=-1) * g_pw
    expert_id = g_sel * MOE_EXPERTS_PER_GROUP + e_idx
    combine = jnp.sum(jax.nn.one_hot(expert_id, MOE_EXPERTS, dtype=F32) * e_w[..., None], axis=-2)
    out = jnp.zeros_like(h)
    for e in range(MOE_EXPERTS):
        he = jax.nn.silu(h @ w_gate[e]) * (h @ w_up[e])
        out = out + combine[..., e:e + 1].astype(h.dtype) * (he @ w_down[e])
    return out

def second_inputs(seed: int = 0) -> dict:
    key = jax.random.key(seed)
    ks = jax.random.split(key, 24)
    nrm = jax.random.normal

    def gain(k, n):
        return 1.0 + 0.02 * nrm(k, (DEPTH_2, n), F32)

    dt0 = jnp.exp(jax.random.uniform(ks[6], (DEPTH_2, SSD_HEADS), F32)
                  * (math.log(0.1) - math.log(1e-3)) + math.log(1e-3))
    return {
        'x': nrm(ks[0], (BATCH, SEQ, D_MODEL), F32),
        'p': nrm(ks[1], (DEPTH_2, BATCH, SEQ, PLE_DIM), F32),
        'mix_norm_g': gain(ks[2], D_MODEL),
        'w_in': nrm(ks[3], (DEPTH_2, D_MODEL, IN_DIM), F32) * D_MODEL ** -0.5,
        'conv_w': nrm(ks[4], (DEPTH_2, SSD_CONV, SSD_CONV_DIM), F32) * SSD_CONV ** -0.5,
        'conv_b': 0.02 * nrm(ks[5], (DEPTH_2, SSD_CONV_DIM), F32),
        'dt_bias': dt0 + jnp.log(-jnp.expm1(-dt0)),
        'a_log': jnp.log(jax.random.uniform(ks[7], (DEPTH_2, SSD_HEADS), F32, minval=1.0, maxval=16.0)),
        'd_skip': gain(ks[8], SSD_HEADS),
        'ssd_norm_g': gain(ks[9], SSD_D_INNER),
        'w_out_a': nrm(ks[10], (DEPTH_2, A_WIDTH, D_MODEL), F32) * A_WIDTH ** -0.5,
        'w_out_b': nrm(ks[11], (DEPTH_2, SSD_D_INNER, D_MODEL), F32) * SSD_D_INNER ** -0.5,
        'w_out': nrm(ks[12], (DEPTH_2, D_MODEL, D_MODEL), F32) * D_MODEL ** -0.5,
        'ffn_norm_g': gain(ks[13], D_MODEL),
        'w_rg': nrm(ks[14], (DEPTH_2, D_MODEL, MOE_GROUPS), F32) * D_MODEL ** -0.5,
        'b_rg': 0.01 * nrm(ks[15], (DEPTH_2, MOE_GROUPS), F32),
        'w_re': nrm(ks[16], (DEPTH_2, D_MODEL, MOE_EXPERTS), F32) * D_MODEL ** -0.5,
        'b_re': 0.01 * nrm(ks[17], (DEPTH_2, MOE_EXPERTS), F32),
        'w_gate': nrm(ks[18], (DEPTH_2, MOE_EXPERTS, D_MODEL, MOE_D_FF), F32) * D_MODEL ** -0.5,
        'w_up': nrm(ks[19], (DEPTH_2, MOE_EXPERTS, D_MODEL, MOE_D_FF), F32) * D_MODEL ** -0.5,
        'w_down': nrm(ks[20], (DEPTH_2, MOE_EXPERTS, MOE_D_FF, D_MODEL), F32) * MOE_D_FF ** -0.5,
        'w_ple_proj': nrm(ks[21], (DEPTH_2, PLE_DIM, D_MODEL), F32) * PLE_DIM ** -0.5,
        'w_ple_gate': nrm(ks[22], (DEPTH_2, D_MODEL, D_MODEL), F32) * D_MODEL ** -0.5,
        'final_norm_g': 1.0 + 0.02 * nrm(ks[23], (D_MODEL,), F32),
    }

def second_block(x, p, mix_norm_g, w_in, conv_w, conv_b, dt_bias, a_log, d_skip, ssd_norm_g,
              w_out_a, w_out_b, w_out, ffn_norm_g, w_rg, b_rg, w_re, b_re, w_gate, w_up,
              w_down, w_ple_proj, w_ple_gate, final_norm_g):
    bsz, s, _ = x.shape
    for i in range(DEPTH_2):
        h = rms_norm(x, mix_norm_g[i])
        proj = h @ w_in[i]
        q = proj[..., OFF_Q:OFF_K].reshape(bsz, s, A_HEADS, A_HEAD_DIM)
        k = proj[..., OFF_K:OFF_V].reshape(bsz, s, A_HEADS, A_HEAD_DIM)
        v = proj[..., OFF_V:OFF_Z].reshape(bsz, s, A_HEADS, A_HEAD_DIM)
        z = proj[..., OFF_Z:OFF_XBC]
        xbc = proj[..., OFF_XBC:OFF_DT]
        dt_raw = proj[..., OFF_DT:OFF_GA]
        gate_a = jax.nn.sigmoid(proj[..., OFF_GA:OFF_GB])
        gate_b = jax.nn.sigmoid(proj[..., OFF_GB:IN_DIM])
        y_a = moba_attention(q, k, v).reshape(bsz, s, A_WIDTH) @ w_out_a[i]
        y_b = ssd_mixer(z, xbc, dt_raw, conv_w[i], conv_b[i], dt_bias[i], a_log[i],
                        d_skip[i], ssd_norm_g[i]) @ w_out_b[i]
        x = x + (gate_a * y_a + gate_b * y_b) @ w_out[i]
        h2 = rms_norm(x, ffn_norm_g[i])
        x = x + hier_moe(h2, w_rg[i], b_rg[i], w_re[i], b_re[i], w_gate[i], w_up[i], w_down[i])
        x = x + jax.nn.sigmoid(x @ w_ple_gate[i]) * (p[i] @ w_ple_proj[i])
    return rms_norm(x, final_norm_g)


def setup_inputs(seed=0):
    out = dict(first_inputs(seed))
    for name, value in second_inputs(seed + 1).items():
        if name != "x":
            out[name + "_2"] = value
    return out


def reference(
    x, mem, w_in, w_a2, b_a, gla_norm_g, w_s, b_s, sgu_ln_g, sgu_ln_b, w_out, wq_x, wk_x, wv_x,
    wo_x, w_router, b_router, w_gate, w_up, w_down, ln_g, ln_b, p_2, mix_norm_g_2, w_in_2,
    conv_w_2, conv_b_2, dt_bias_2, a_log_2, d_skip_2, ssd_norm_g_2, w_out_a_2, w_out_b_2,
    w_out_2, ffn_norm_g_2, w_rg_2, b_rg_2, w_re_2, b_re_2, w_gate_2, w_up_2, w_down_2,
    w_ple_proj_2, w_ple_gate_2, final_norm_g_2,
):
    x = first_block(
        x, mem, w_in, w_a2, b_a, gla_norm_g, w_s, b_s, sgu_ln_g, sgu_ln_b, w_out, wq_x, wk_x,
        wv_x, wo_x, w_router, b_router, w_gate, w_up, w_down, ln_g, ln_b,
    )
    return second_block(
        x, p_2, mix_norm_g_2, w_in_2, conv_w_2, conv_b_2, dt_bias_2, a_log_2, d_skip_2,
        ssd_norm_g_2, w_out_a_2, w_out_b_2, w_out_2, ffn_norm_g_2, w_rg_2, b_rg_2, w_re_2,
        b_re_2, w_gate_2, w_up_2, w_down_2, w_ple_proj_2, w_ple_gate_2, final_norm_g_2,
    )


_drawn_inputs = setup_inputs


def setup_inputs(seed=0):
    import zlib

    import numpy as np

    out = dict(_drawn_inputs(seed))
    spreads = {}
    factors = {'d_skip_2': 5.133,
     'ssd_norm_g_2': 3.056,
     'ffn_norm_g_2': 2.682,
     'b_rg_2': 4.382,
     'b_re_2': 8.0,
     'final_norm_g_2': 2.857}
    for name, (base, spread) in spreads.items():
        noise = np.random.default_rng([zlib.crc32(name.encode()), seed]).standard_normal(out[name].shape)
        drawn = base * np.exp(spread * noise) if base else spread * noise
        out[name] = jnp.asarray(drawn.astype(out[name].dtype))
    for name, factor in factors.items():
        out[name] = (out[name] * factor).astype(out[name].dtype)
    return out
```

```python
from contextlib import ExitStack

import concourse.bass as bass
from concourse import mybir

F32 = mybir.dt.float32
F32R = mybir.dt.float32r
ACT = mybir.ActivationFunctionType
ALU = mybir.AluOpType
AX = mybir.AxisListType.X

P = 128
CHUNK_COLS = 2048
RAW = 6
SPLIT = 2
SLOTS = 4
NEG = -1.0e30


class Counter:

    def __init__(self, eng, sem):
        self.eng, self.sem, self.n = eng, sem, 0

    def link(self, ins):
        self.n += 1
        ins.then_inc(self.sem, 1)
        self.eng.wait_ge(self.sem, self.n)


def build(nc, a, out):
    DEPTH, D = a["w_in"].shape[0], a["w_in"].shape[1]
    T = a["x"].shape[1]
    TT = T // P
    KC = D // P
    NE, FF = a["w_gate"].shape[1], a["w_gate"].shape[3]
    FC = FF // P
    DQK = a["w_a2"].shape[2]
    DGLA = a["gla_norm_g"].shape[1]
    RANK = a["w_a2"].shape[1]
    DSGU = a["sgu_ln_g"].shape[1]
    GH = 4
    DK, DV = DQK // GH, DGLA // GH
    LCH = 64
    SG = a["w_s"].shape[1]
    XH = 4
    XD = D // XH
    ALPHA = (2.0 * DEPTH) ** 0.25
    LN_EPS, RMS_EPS = 1e-5, 1e-6
    GATE_TEMP = 16.0
    AH, AD = 8, 64
    SH = a["a_log_2"].shape[1]
    SP = D // SH
    SGR = 2
    CONV = a["conv_w_2"].shape[1]
    CDIM = a["conv_w_2"].shape[2]
    CB = CDIM // P
    XB_BLOCKS = CDIM // 512
    PLE = a["p_2"].shape[3]
    PAIRS = GH // 2
    NCH = T // LCH

    O_Q, O_V, O_R, O_A = 0, 2 * DQK, 2 * DQK + DGLA, 2 * DQK + 2 * DGLA
    O_U = O_A + RANK
    O_VS = O_U + DSGU
    O_Q2, O_K2, O_V2, O_Z2, O_XB2 = 0, 512, 1024, 1536, 1536 + D
    O_DT2 = O_XB2 + CDIM
    O_GA2 = O_DT2 + SH
    O_GB2 = O_GA2 + D

    def cols(w, c0, j):
        return w.rearrange("(p c) n -> p c n", p=P)[:, 4 * j:4 * j + 4, c0:c0 + 512]

    def rows_pc(w, j):
        return w.rearrange("(p c) n -> p c n", p=P)[:, 2 * j:2 * j + 2, :]

    def rows_cp(w, j):
        return w.rearrange("(c p) n -> p c n", p=P)[:, 2 * j:2 * j + 2, :]

    stream = []
    n_chunks = 0
    last_of_job = {}
    plain_before = {}
    plain = 0
    job = {}
    turns = [0] * SLOTS
    next_slot = 0
    moe_at = []

    def plan_job(*names):
        nonlocal next_slot
        for name in names:
            job[name] = (next_slot, turns[next_slot])
            turns[next_slot] += 1
            next_slot = (next_slot + 1) % SLOTS

    def plan_dense(sources, *names):
        nonlocal n_chunks, plain
        plan_job(*names)
        for k, s in enumerate(sources):
            stream.append(s)
            plain_before[n_chunks] = plain
            if k == len(sources) - 1:
                last_of_job[n_chunks] = names[-1]
            else:
                plain += 1
            n_chunks += 1

    G_SLOT, U_SLOT, T_SLOT, Y0_SLOT = 0, 1, 2, 3
    TURNS_PER_EXPERT = (1, 1, 2, 1)

    def plan_moe(gate, up, down):
        nonlocal n_chunks, plain, next_slot
        moe_at.append((n_chunks, list(turns), plain))
        stream.append(("experts", gate, up, down))
        n_chunks += 6 * NE
        plain += 3 * NE
        for s in range(SLOTS):
            turns[s] += TURNS_PER_EXPERT[s] * NE
        next_slot = 0

    plan_job("colc")
    for l in range(DEPTH):
        L = f"{l}."
        plan_job(L + "xT0", L + "xT1")
        w = a["w_in"][l]
        for name, c0 in (("qk", O_Q), ("v", O_V), ("r", O_R), ("u", O_U), ("vs", O_VS)):
            plan_dense([cols(w, c0, j) for j in range(2)], L + name)
        plan_job(L + "a", L + "wsT", L + "qT", L + "aT", L + "z", L + "mix_sgu", L + "decay", L + "kv0", L + "kv1",
                 L + "o0", L + "o1")
        plan_job(L + "yT0", L + "yT1")
        plan_dense([rows_pc(a["w_out"][l], j) for j in range(4)], L + "h0", L + "h1")
        plan_job(L + "memT0", L + "memT1")
        for b in range(2):
            plan_dense([cols(a["wk_x"][l], 512 * b, j) for j in range(2)], L + f"k{b}a", L + f"k{b}b")
        plan_dense([rows_pc(a["wv_x"][l], j) for j in range(4)], L + "xv0", L + "xv1")
        plan_job(L + "x1T0", L + "x1T1")
        for b in range(2):
            plan_dense([cols(a["wq_x"][l], 512 * b, j) for j in range(2)], L + f"q{b}a", L + f"q{b}b")
        plan_job(L + "s0", L + "s1", L + "pT0", L + "pT1", L + "oT0", L + "oT1")
        plan_dense([rows_cp(a["wo_x"][l], j) for j in range(4)], L + "xh0", L + "xh1")
        plan_job(L + "x2T0", L + "x2T1", L + "router")
        plan_moe(a["w_gate"][l], a["w_up"][l], a["w_down"][l])
    w = a["w_in_2"][0]
    plan_job("2.xT0", "2.xT1")
    for name, c0 in (("q", O_Q2), ("k", O_K2)):
        plan_dense([cols(w, c0, j) for j in range(2)], f"2.{name}a", f"2.{name}b")
    plan_dense([cols(w, O_V2, j) for j in range(2)], "2.v")
    for b in range(XB_BLOCKS):
        plan_dense([cols(w, O_XB2 + 512 * b, j) for j in range(2)], f"2.xb{b}a", f"2.xb{b}b")
    for name, c0 in (("z", O_Z2), ("ga", O_GA2), ("gb", O_GB2)):
        for b in range(2):
            plan_dense([cols(w, c0 + 512 * b, j) for j in range(2)], f"2.{name}{b}")
    plan_job("2.dt")
    for k in range(AH // 2):
        plan_job(f"2.s{k}", f"2.pT{k}", f"2.oT{k}")
    plan_dense([rows_cp(a["w_out_a_2"][0], j) for j in range(2)], "2.ya0", "2.ya1")
    plan_job("2.cs", "2.csT", "2.cb", "2.xs0", "2.xs1")
    HB = 4
    for k in range(SH // HB):
        plan_job(f"2.csb{k}")
        plan_job(f"2.y{k}")
    plan_job("2.uT0", "2.uT1")
    plan_dense([rows_pc(a["w_out_b_2"][0], j) for j in range(4)], "2.yb0", "2.yb1")
    plan_job("2.mT0", "2.mT1")
    plan_dense([rows_pc(a["w_out_2"][0], j) for j in range(4)], "2.h0", "2.h1")
    plan_job("2.x1T0", "2.x1T1", "2.router")
    plan_moe(a["w_gate_2"][0], a["w_up_2"][0], a["w_down_2"][0])
    plan_job("2.pT")
    plan_dense([a["w_ple_proj_2"][0].rearrange("(p c) n -> p c n", p=P)], "2.pp0", "2.pp1")
    plan_job("2.x2T0", "2.x2T1")
    plan_dense([rows_pc(a["w_ple_gate_2"][0], j) for j in range(4)], "2.pg0", "2.pg1")
    N_CHUNKS = n_chunks

    with ExitStack() as ctx:
        def sb(name, shape, dt=F32):
            return ctx.enter_context(nc.sbuf_tensor(name, shape, dt))

        def sem(name):
            return ctx.enter_context(nc.semaphore(name))

        raw = sb("raw", [P, RAW, CHUNK_COLS])
        w_high = sb("w_high", [P, SPLIT, CHUNK_COLS], F32R)
        w_low = sb("w_low", [P, SPLIT, CHUNK_COLS], F32R)
        act_high = sb("act_high", [P, KC, T], F32R)
        act_low = sb("act_low", [P, KC, T], F32R)
        aux_high = sb("aux_high", [P, KC, T], F32R)
        aux_low = sb("aux_low", [P, KC, T], F32R)
        x = sb("x_res", [P, TT, D])
        W0, W1, W2, W3 = (sb(f"work{i}", [P, 2048]) for i in range(4))
        GA, GB = sb("gate_a", [P, 2048]), sb("gate_b", [P, 2048])
        XB = sb("xbc", [P, CB * T])
        norm_p = sb("norm_params", [P, 2, D])
        ident = sb("ident", [P, P])
        tri = sb("tri", [P, TT, T])
        dist = sb("dist", [P, P + T])
        later = sb("later", [P, P])
        half = sb("half", [P, 2])
        NARROW = DEPTH * RANK + 2 * NE + SH + 4
        nar_high = sb("nar_high", [P, KC, NARROW], F32R)
        nar_low = sb("nar_low", [P, KC, NARROW], F32R)
        colc = sb("colc", [P, (CONV + 1) * CB + DEPTH * SG])
        bias = sb("bias", [P, 16 + 20 + 3 * SH])
        st = sb("stats", [P, 672])
        csT = sb("csT", [SH, T])
        ps = ctx.enter_context(nc.psum_tensor("ps", [P, 2 * SLOTS, 512], F32))

        loaded = [sem(f"loaded{i}") for i in range(RAW)]
        high_ready, low_ready, chunk_used = sem("high_ready"), sem("low_ready"), sem("chunk_used")
        filled = [sem(f"filled{i}") for i in range(SLOTS)]
        free = [sem(f"free{i}") for i in range(SLOTS)]
        names = """x_loaded small_loaded narrow_loaded norm_loaded mixp_loaded mem_loaded rows_loaded p_loaded
            consts_ready narrow_high narrow_ready act_chain dve_chain pool_chain turned_high normed
            srg_ready soft_ready kdec_ready osq_ready vnorm_ready ymix_ready
            smax_ready exp_ready p_ready router_max router_exp moe_added
            conv_done xbc_ready dt_soft dt_ready e_ready m_ready u_ready usq_ready m2_ready
            arg_ready arg_exp stored""".split()
        S = {n: sem(n) for n in names}

        def slot_ps(name):
            s = job[name][0]
            return ps[:, 2 * s:2 * s + 2, :].rearrange("p b n -> p (b n)")

        def slot_banks(name):
            s = job[name][0]
            return ps[:, 2 * s:2 * s + 2, :]

        def wait_full(eng, name):
            slot, turn = job[name]
            eng.wait_ge(filled[slot], turn + 1)

        def wait_released(eng, name):
            slot, turn = job[name]
            eng.wait_ge(free[slot], turn + 1)

        def frees(ins, name):
            ins.then_inc(free[job[name][0]], 1)

        def wait_chunk_used(eng, n):
            if n in last_of_job:
                wait_full(eng, last_of_job[n])
            else:
                eng.wait_ge(chunk_used, plain_before[n] + 1)

        def moe_chunk_used(eng, m, i, j):
            _, at, before = moe_at[m]
            if j % 2 == 0:
                eng.wait_ge(chunk_used, before + 3 * i + j // 2 + 1)
            elif j == 1:
                eng.wait_ge(filled[G_SLOT], at[G_SLOT] + i + 1)
            elif j == 3:
                eng.wait_ge(filled[U_SLOT], at[U_SLOT] + i + 1)
            else:
                eng.wait_ge(filled[T_SLOT], at[T_SLOT] + 2 * i + 2)

        moe_chunks = {n0 + k: m for m, (n0, _, _) in enumerate(moe_at) for k in range(6 * NE)}

        def wait_used_any(eng, n):
            if n in moe_chunks:
                k = n - moe_at[moe_chunks[n]][0]
                moe_chunk_used(eng, moe_chunks[n], k // 6, k % 6)
            else:
                wait_chunk_used(eng, n)

        N_A = [l * RANK for l in range(DEPTH)]
        N_R = DEPTH * RANK
        N_DT = N_R + NE
        N_RE = N_DT + SH
        nar_raw = W3[:, 0:KC * NARROW].rearrange("p (c n) -> p c n", c=KC)
        b_router = bias[:, 0:16]
        b_re = bias[:, 16:36]
        dt_bias = bias[:, 36:36 + SH]
        neg_a = bias[:, 36 + SH:36 + 2 * SH]
        d_skip = bias[:, 36 + 2 * SH:36 + 3 * SH]
        rows_raw = W2[0:colc.shape[1], 0:P]
        conv_w = [colc[:, k * CB:(k + 1) * CB] for k in range(CONV)]
        conv_b = colc[:, CONV * CB:(CONV + 1) * CB]
        b_s = [colc[:, (CONV + 1) * CB + l * SG:(CONV + 1) * CB + (l + 1) * SG] for l in range(DEPTH)]

        qk = W0[:, 0:1024].rearrange("p (t n) -> p t n", t=TT)
        v_gla = W0[:, 1024:2048].rearrange("p (t n) -> p t n", t=TT)
        silu_r = W1[:, 0:1024].rearrange("p (t n) -> p t n", t=TT)
        gelu_u = W1[:, 1024:2048].rearrange("p (t n) -> p t n", t=TT)
        gelu_v = W2[:, 0:1024].rearrange("p (t n) -> p t n", t=TT)
        log_a = W2[:, 1024:1536].rearrange("p (t n) -> p t n", t=TT)
        k_dec = W2[:, 1536:2048].rearrange("p (t n) -> p t n", t=TT)
        ymix = W3[:].rearrange("p (t n) -> p t n", t=TT)
        state = GA[:, 0:1024].rearrange("p (a c n) -> p a c n", a=PAIRS, c=NCH)
        soft = GA[:, 1024:1536].rearrange("p (t n) -> p t n", t=TT)
        a_tok = GA[:, 1536:1536 + TT * RANK].rearrange("p (t n) -> p t n", t=TT)
        aT = GA[0:RANK + 1, 1600:1600 + T]
        qT_gla = GB[:, 0:512].rearrange("p (a t) -> p a t", a=PAIRS)
        wsT = GB[:, 512:1024].rearrange("p (g t) -> p g t", g=SG)
        ws_raw = GB[:, 1024:1536].rearrange("p (g t) -> p g t", g=SG)
        osq = GB[:, 1024:2048].rearrange("p (t b n) -> p t b n", t=TT, b=2)
        gn_g, sln_g, sln_b = (XB[:, 512 * i:512 * i + 512] for i in range(3))
        w_a2 = XB[0:RANK + 1, 1536:1536 + DQK]
        summed = GA[:].rearrange("p (t n) -> p t n", t=TT)
        mem_tok = GB[:].rearrange("p (t n) -> p t n", t=TT)
        kT = W1[:].rearrange("p (f m) -> p f m", f=KC)
        xv = W2[:].rearrange("p (t n) -> p t n", t=TT)
        qT = W0[:].rearrange("p (f t) -> p f t", f=KC)
        prob = W3[:].rearrange("p (t h m) -> p t h m", t=TT, h=XH)
        pT = GA[:].rearrange("p (h b t) -> p h b t", h=XH, b=TT)
        silu_g = W0[:, 0:1024].rearrange("p (t n) -> p t n", t=TT)
        hid = W0[:, 1024:2048].rearrange("p (t n) -> p t n", t=TT)
        y_acc = W1[:].rearrange("p (t n) -> p t n", t=TT)
        gates = st[:, 512:512 + TT * NE].rearrange("p (t n) -> p t n", t=TT)

        def stat(at, *shape):
            n = 1
            for k in shape:
                n *= k
            flat = st[:, at:at + n]
            if len(shape) == 1:
                return flat
            dims = " ".join("abcd"[:len(shape)])
            return flat.rearrange(f"p ({dims}) -> p {dims}", **dict(zip("abcd", shape)))

        bn, mean_var, rstd = stat(0, TT, 2, 6), stat(24, TT, 2), stat(28, TT, 1)
        chunk_decay = stat(32, PAIRS, NCH)
        o_ms, o_rs = stat(40, TT, GH), stat(48, TT, GH)
        v_bn, v_mv, v_rstd = stat(64, TT, SG, 6), stat(112, TT, SG, 2), stat(128, TT, SG, 1)
        neg_max, p_sum, p_inv = stat(136, TT, XH), stat(144, TT, XH), stat(152, TT, XH)
        logits = stat(160, TT, NE + 4)
        rank, beat, top = stat(200, TT, 4, 4), stat(232, TT, 4, 4), stat(264, TT, 4, 4)
        r_max, r_sum, r_inv = stat(296, TT, 1), stat(298, TT, 1), stat(300, TT, 1)
        g_score, g_max, g_eq = stat(304, TT, 4), stat(312, TT, 1), stat(316, TT, 4)
        g_seen, g_first = stat(324, TT, 4), stat(332, TT, 4)
        probs = stat(340, TT, NE)
        g_prob, e_max, e_pick, m_sel = stat(372, TT, 4), stat(380, TT, 4), stat(388, TT, 4), stat(396, TT, 1)
        dt_in, dt_soft, dt = stat(400, TT, SH), stat(432, TT, SH), stat(464, TT, SH)
        da, cs = stat(544, TT, SH), stat(576, TT, SH)
        neg_max2, p_sum2, p_inv2 = stat(608, TT, 2), stat(612, TT, 2), stat(616, TT, 2)
        u_ms, u_rs = stat(620, TT, SGR), stat(624, TT, SGR)

        h_tok = W0[:].rearrange("p (t n) -> p t n", t=TT)
        q2T = W1[:, 0:1024].rearrange("p (f t) -> p f t", f=4)
        k2T = W1[:, 1024:2048].rearrange("p (f t) -> p f t", f=4)
        v2 = W2[:, 0:1024].rearrange("p (t n) -> p t n", t=TT)
        p2 = [W0[:, 1024 * k:1024 * k + 768].rearrange("p (h n) -> p h n", h=2) for k in range(2)]
        p2T = W2[:, 1024:1792].rearrange("p (h n) -> p h n", h=2)
        zs = W3[:].rearrange("p (t n) -> p t n", t=TT)
        PADW = T + CONV - 1
        pad = [(GA, GB)[k][:, 0:4 * PADW].rearrange("p (b t) -> p b t", b=4) for k in range(2)]
        xbcT = XB[:].rearrange("p (b t) -> p b t", b=CB)
        ga = GA[:].rearrange("p (t n) -> p t n", t=TT)
        gb = GB[:].rearrange("p (t n) -> p t n", t=TT)
        xs = W0[:].rearrange("p (t n) -> p t n", t=TT)
        xdt = W1[:].rearrange("p (t n) -> p t n", t=TT)
        decay2 = W2[:, 0:HB * 384].rearrange("p (h n) -> p h n", h=HB)
        cbT = XB[:, 0:768].rearrange("p (g n) -> p g n", g=SGR)
        usq = XB[:, 768:768 + 2048].rearrange("p (t n) -> p t n", t=TT)
        p_tok = W3[:, 0:TT * PLE].rearrange("p (t n) -> p t n", t=TT)
        pp = W2[:].rearrange("p (t n) -> p t n", t=TT)
        sig = W3[:].rearrange("p (t n) -> p t n", t=TT)

        def bcast(vec, n):
            return vec.rearrange("(a n) -> a n", a=1).to_broadcast([P, n])

        norms = [(a["ln_g"][l, k], a["ln_b"][l, k]) for l in range(DEPTH) for k in range(3)]
        norms += [(a[k][0] if k != "final_norm_g_2" else a[k], None)
                  for k in ("mix_norm_g_2", "ssd_norm_g_2", "ffn_norm_g_2", "final_norm_g_2")]
        norm_need = []
        for g, b in norms:
            norm_need.append((norm_need[-1] if norm_need else 0) + (16 if b is None else 32))

        block = ctx.enter_context(nc.Block())

        @block.sync
        def _(sp):
            sp.dma_start(x[:], a["x"][0].rearrange("(t p) n -> p t n", p=P)).then_inc(S["x_loaded"], 16)
            n, m = 0, 0

            def load(n, src):
                if n >= RAW:
                    sp.wait_ge(low_ready, n - RAW + 1)
                dst = raw[:, n % RAW, :].rearrange("p (c n) -> p c n", c=src.shape[1])
                sp.dma_start(dst, src).then_inc(loaded[n % RAW], 16)

            for src in stream:
                if not isinstance(src, tuple):
                    load(n, src)
                    n += 1
                    continue
                _, gate, up, down = src
                with sp.Fori(0, NE) as e:
                    for j in range(6):
                        w = (gate, up, down)[j // 2][bass.ds(e, 1)]
                        c = w.shape[1] // P // 2
                        src_j = w.rearrange("e (p c) n -> p (e c) n", p=P)[:, c * (j % 2):c * (j % 2) + c, :]
                        sp.wait_ge(low_ready, 6 * e + (n + j - RAW + 1))
                        dst = raw[:, (n + j) % RAW, :].rearrange("p (c n) -> p c n", c=c)
                        sp.dma_start(dst, src_j).then_inc(loaded[(n + j) % RAW], 16)
                n += 6 * NE
                m += 1
            sp.wait_ge(S["normed"], len(norms))
            sp.dma_start(out[0].rearrange("(t p) n -> p t n", p=P), sig[:]).then_inc(S["stored"], 16)
            sp.wait_ge(S["stored"], 16)

        @block.gpsimd
        def _(pool):
            chain = Counter(pool, S["pool_chain"])
            with nc.allow_non_contiguous_dma(reason="narrow weight columns, loaded once"):
                c0 = 0
                for w, k0, k in ([(a["w_in"][l], O_A, RANK) for l in range(DEPTH)]
                                 + [(a["w_router"], 0, NE), (a["w_in_2"][0], O_DT2, SH),
                                    (a["w_re_2"][0], 0, NE), (a["w_rg_2"][0], 0, 4)]):
                    src = w.rearrange("(p c) n -> p c n", p=P)[:, :, k0:k0 + k]
                    pool.dma_start(nar_raw[:, :, c0:c0 + k], src).then_inc(S["narrow_loaded"], 16)
                    c0 += k
            nconv = CONV * CB
            pool.dma_start(rows_raw[0:nconv], a["conv_w_2"][0].rearrange("k (b p) -> (k b) p", p=P)).then_inc(S["rows_loaded"], 16)
            pool.dma_start(rows_raw[nconv:nconv + CB], a["conv_b_2"][0].rearrange("(b p) -> b p", p=P)).then_inc(S["rows_loaded"], 16)
            pool.dma_start(rows_raw[nconv + CB:nconv + CB + DEPTH * SG], a["b_s"].rearrange("l g p -> (l g) p")).then_inc(S["rows_loaded"], 16)
            for dst, vec in ((b_router, a["b_router"]), (b_re[:, 0:NE], a["b_re_2"][0]), (b_re[:, NE:NE + 4], a["b_rg_2"][0]),
                             (dt_bias, a["dt_bias_2"][0]), (neg_a, a["a_log_2"][0]), (d_skip, a["d_skip_2"][0])):
                pool.dma_start(dst, bcast(vec, vec.shape[0])).then_inc(S["small_loaded"], 16)

            def load_mix_params(l):
                for dst, vec in ((gn_g, a["gla_norm_g"]), (sln_g, a["sgu_ln_g"]), (sln_b, a["sgu_ln_b"])):
                    pool.dma_start(dst, bcast(vec[l], 512)).then_inc(S["mixp_loaded"], 16)
                pool.dma_start(w_a2[0:RANK], a["w_a2"][l]).then_inc(S["mixp_loaded"], 16)
                pool.dma_start(w_a2[RANK:RANK + 1], a["b_a"][l].rearrange("(a n) -> a n", a=1)).then_inc(S["mixp_loaded"], 16)
                pool.dma_start(ws_raw, a["w_s"][l].rearrange("g t s -> t g s")).then_inc(S["mixp_loaded"], 16)

            def load_norm(k):
                if k:
                    pool.wait_ge(S["normed"], k)
                g, b = norms[k]
                pool.dma_start(norm_p[:, 0, :], bcast(g, D)).then_inc(S["norm_loaded"], 16)
                if b is not None:
                    pool.dma_start(norm_p[:, 1, :], bcast(b, D)).then_inc(S["norm_loaded"], 16)

            chain.link(nc.gpsimd.memset(ident[:], 0.0))
            chain.link(nc.gpsimd.affine_select(ident[:], ident[:], [[-1, P]], ALU.not_equal, 1.0, base=0, channel_multiplier=1))
            chain.link(nc.gpsimd.memset(tri[:], 1.0))
            for t in range(TT):
                chain.link(nc.gpsimd.affine_select(tri[:, t, :], tri[:, t, :], [[1, T]], ALU.is_ge, 0.0, base=-P * t, channel_multiplier=-1))
            for t in range(TT):
                at = dist[:, 0:P] if t == 0 else dist[:, P:P + T]
                chain.link(nc.gpsimd.iota(at, [[1, P * (t + 1)]], base=-P * t, channel_multiplier=-1, allow_small_or_imprecise_dtypes=True))
                chain.link(nc.gpsimd.affine_select(at, at, [[-1, P * (t + 1)]], ALU.is_ge, NEG, base=P * t, channel_multiplier=1))
            chain.link(nc.gpsimd.memset(later[:], 1.0))
            chain.link(nc.gpsimd.affine_select(later[:], later[:], [[-1, P]], ALU.is_gt, 0.0, base=0, channel_multiplier=1))
            chain.link(nc.gpsimd.memset(later[LCH:P, 0:LCH], 0.0))
            chain.link(nc.gpsimd.memset(half[:], 0.0))
            chain.link(nc.gpsimd.memset(half[0:LCH, 0:1], 1.0))
            chain.link(nc.gpsimd.memset(half[LCH:P, 1:2], 1.0))
            nc.gpsimd.memset(st[:], 0.0).then_inc(S["consts_ready"], 1)
            load_norm(0)
            for l in range(DEPTH):
                if l:
                    pool.wait_ge(S["normed"], 3 * l)
                load_mix_params(l)
                wait_released(pool, f"{l}.r")
                pool.wait_ge(S["mixp_loaded"], 96 * (l + 1))
                for t in range(TT):
                    nc.gpsimd.tensor_tensor(silu_r[:, t, :], silu_r[:, t, :], gn_g, ALU.mult).then_inc(S["srg_ready"], 1)
                pool.wait_ge(S["ymix_ready"], l + 1)
                pool.dma_start(mem_tok, a["mem"][0].rearrange("(t p) n -> p t n", p=P)).then_inc(S["mem_loaded"], 16)
                load_norm(3 * l + 1)
                load_norm(3 * l + 2)
                load_norm(3 * l + 3)
            load_norm(3 * DEPTH + 1)
            load_norm(3 * DEPTH + 2)
            load_norm(3 * DEPTH + 3)
            pool.wait_ge(S["m2_ready"], 1)
            pool.dma_start(p_tok, a["p_2"][0, 0].rearrange("(t p) n -> p t n", p=P)).then_inc(S["p_loaded"], 16)

        @block.tensor
        def _(pe):
            n = 0

            def begin(name):
                slot, turn = job[name]
                if turn:
                    pe.wait_ge(free[slot], turn)

            def full(ins, name):
                ins.then_inc(filled[job[name][0]], 1)

            def three(out, hl_l, hl_r, first, last):
                (lh, ll), (rh, rl) = hl_l, hl_r
                pe.matmul(out, lh, rh, start=first, stop=False)
                pe.matmul(out, lh, rl, start=False, stop=False)
                return pe.matmul(out, ll, rh, start=False, stop=last)

            def chunk_split(n):
                pe.wait_ge(low_ready, n + 1)

            def weights(n, lo, hi):
                return w_high[:, n % SPLIT, lo:hi], w_low[:, n % SPLIT, lo:hi]

            def operand(pair, c, lo, hi):
                return pair[0][:, c, lo:hi], pair[1][:, c, lo:hi]

            MAIN, AUX = (act_high, act_low), (aux_high, aux_low)

            def dense_cols(name, src=MAIN):
                nonlocal n
                begin(name)
                bank = slot_banks(name)
                for j in range(2):
                    chunk_split(n)
                    for c in range(4):
                        for t in range(TT):
                            k = 4 * j + c
                            i = three(bank[:, t, :], operand(src, k, t * P, t * P + P), weights(n, 512 * c, 512 * c + 512),
                                      k == 0, k == KC - 1)
                    if j == 0:
                        i.then_inc(chunk_used, 1)
                    n += 1
                full(i, name)

            def dense_rows(names, chunks, src=MAIN, per=2):
                nonlocal n
                for t in range(TT):
                    begin(names[t])
                last = chunks * per - 1
                for j in range(chunks):
                    chunk_split(n)
                    for t in range(TT):
                        for c in range(per):
                            for b in range(2):
                                k = per * j + c
                                i = three(slot_banks(names[t])[:, b, :], operand(src, k, t * P, t * P + P),
                                          weights(n, 1024 * c + 512 * b, 1024 * c + 512 * b + 512), k == 0, k == last)
                        if j == chunks - 1:
                            full(i, names[t])
                    if j < chunks - 1:
                        i.then_inc(chunk_used, 1)
                    n += 1

            def dense_turned(name, src=MAIN):
                nonlocal n
                begin(name + "a")
                begin(name + "b")
                for j in range(2):
                    chunk_split(n)
                    for f in range(4):
                        bank = slot_banks(name + "ab"[f // 2])[:, f % 2, 0:T]
                        for c in range(4):
                            k = 4 * j + c
                            i = three(bank, weights(n, 512 * c + P * f, 512 * c + P * f + P), operand(src, k, 0, T),
                                      k == 0, k == KC - 1)
                        if j == 1 and f % 2 == 1:
                            full(i, name + "ab"[f // 2])
                    if j == 0:
                        i.then_inc(chunk_used, 1)
                    n += 1

            def turn(src, names, width=D):
                C = width // P
                for k, name in enumerate(names):
                    begin(name)
                    dst = slot_ps(name).rearrange("p (c t) -> p c t", t=T)
                    for c in range(C // len(names)):
                        cc = k * (C // len(names)) + c
                        for t in range(TT):
                            i = pe.transpose(dst[:, c, t * P:t * P + P], src[:, t, cc::C], ident[:])
                    full(i, name)

            def narrow(name, c0, width):
                begin(name)
                dst = slot_ps(name)
                for t in range(TT):
                    for c in range(KC):
                        i = three(dst[:, t * width:t * width + width], operand(MAIN, c, t * P, t * P + P),
                                  (nar_high[:, c, c0:c0 + width], nar_low[:, c, c0:c0 + width]), c == 0, c == KC - 1)
                full(i, name)

            def experts(m):
                nonlocal n
                n0, at, _ = moe_at[m]
                G, U, TS, Y0 = (ps[:, 2 * s:2 * s + 2, :] for s in range(SLOTS))
                with pe.Fori(0, NE) as e:
                    for part, (slot, dst) in enumerate(((G_SLOT, G), (U_SLOT, U))):
                        if at[slot]:
                            pe.wait_ge(free[slot], e + at[slot])
                        for j in range(2):
                            k = 2 * part + j
                            pe.wait_ge(low_ready, 6 * e + (n0 + k + 1))
                            for c in range(4):
                                for t in range(TT):
                                    i = three(dst[:, t, :], operand(MAIN, 4 * j + c, t * P, t * P + P),
                                              weights(n0 + k, 512 * c, 512 * c + 512), 4 * j + c == 0, 4 * j + c == KC - 1)
                            i.then_inc(chunk_used if j == 0 else filled[slot], 1)
                    pe.wait_ge(free[U_SLOT], e + (at[U_SLOT] + 1))
                    pe.wait_ge(free[T_SLOT], 2 * e + at[T_SLOT])
                    dst = TS.rearrange("p b n -> p (b n)").rearrange("p (c t) -> p c t", t=T)
                    for c in range(FC):
                        for t in range(TT):
                            i = pe.transpose(dst[:, c, t * P:t * P + P], hid[:, t, c::FC], ident[:])
                    i.then_inc(filled[T_SLOT], 1)
                    pe.wait_ge(free[T_SLOT], 2 * e + (at[T_SLOT] + 1))
                    pe.wait_ge(free[Y0_SLOT], e + at[Y0_SLOT])
                    for j in range(2):
                        pe.wait_ge(low_ready, 6 * e + (n0 + 4 + j + 1))
                        for t in range(TT):
                            for c in range(2):
                                for b in range(2):
                                    k = 2 * j + c
                                    i = three((Y0, TS)[t][:, b, :], operand(AUX, k, t * P, t * P + P),
                                              weights(n0 + 4 + j, 1024 * c + 512 * b, 1024 * c + 512 * b + 512), k == 0, k == FC - 1)
                            if j == 1:
                                i.then_inc(filled[(Y0_SLOT, T_SLOT)[t]], 1)
                        if j == 0:
                            i.then_inc(chunk_used, 1)
                n = n0 + 6 * NE

            def operand_ready(*names):
                for name in names:
                    wait_released(pe, name)

            pe.wait_ge(S["consts_ready"], 1)
            begin("colc")
            pe.wait_ge(S["rows_loaded"], 48)
            rows_n = colc.shape[1]
            full(pe.transpose(slot_ps("colc")[:, 0:rows_n], rows_raw, ident[0:rows_n, 0:rows_n]), "colc")
            pe.wait_ge(S["x_loaded"], 16)
            for l in range(DEPTH):
                L = f"{l}."
                if l:
                    pe.wait_ge(S["normed"], 3 * l)
                turn(x, (L + "xT0", L + "xT1"))
                operand_ready(L + "xT0", L + "xT1")
                for name in ("qk", "v", "r", "u", "vs"):
                    dense_cols(L + name)
                pe.wait_ge(S["narrow_ready"], 1)
                narrow(L + "a", N_A[l], RANK)
                begin(L + "wsT")
                pe.wait_ge(S["mixp_loaded"], 96 * (l + 1))
                for g in range(SG):
                    i = pe.transpose(slot_ps(L + "wsT")[:, g * P:g * P + P], ws_raw[:, g, :], ident[:])
                full(i, L + "wsT")
                begin(L + "qT")
                wait_released(pe, L + "qk")
                for k in range(PAIRS):
                    for t in range(TT):
                        i = pe.transpose(slot_ps(L + "qT")[:, k * T + t * P:k * T + t * P + P], qk[:, t, k * P:k * P + P], ident[:])
                full(i, L + "qT")
                begin(L + "aT")
                wait_released(pe, L + "a")
                for t in range(TT):
                    i = pe.transpose(slot_ps(L + "aT")[0:RANK, t * P:t * P + P], a_tok[:, t, :], ident[:])
                full(i, L + "aT")
                begin(L + "z")
                wait_released(pe, L + "aT")
                for t in range(TT):
                    i = pe.matmul(slot_ps(L + "z")[:, t * DQK:t * DQK + DQK], aT[:, t * P:t * P + P], w_a2, start=True, stop=True)
                full(i, L + "z")
                begin(L + "mix_sgu")
                wait_released(pe, L + "wsT")
                pe.wait_ge(S["vnorm_ready"], l + 1)
                for t in range(TT):
                    for g in range(SG):
                        i = pe.matmul(slot_banks(L + "mix_sgu")[:, t, g * P:g * P + P], wsT[:, g, :], gelu_v[:, t, g * P:g * P + P], start=True, stop=True)
                full(i, L + "mix_sgu")
                begin(L + "decay")
                wait_released(pe, L + "z")
                for t in range(TT):
                    pe.matmul(slot_banks(L + "decay")[:, 0, t * DQK:t * DQK + DQK], later[:], log_a[:, t, :], start=True, stop=True)
                for k in range(PAIRS):
                    for t in range(TT):
                        i = pe.matmul(slot_banks(L + "decay")[:, 1, 4 * k + 2 * t:4 * k + 2 * t + 2], log_a[:, t, k * P:k * P + P], half[:], start=True, stop=True)
                full(i, L + "decay")
                pe.wait_ge(S["kdec_ready"], l + 1)
                wait_released(pe, L + "v")
                for k in range(PAIRS):
                    begin(L + f"kv{k}")
                    for c in range(NCH):
                        t, hf = c // 2, c % 2
                        rows = slice(LCH * hf, LCH * hf + LCH)
                        i = pe.matmul(slot_banks(L + f"kv{k}")[:, hf, 256 * t:256 * t + 256], k_dec[rows, t, k * P:k * P + P],
                                      v_gla[rows, t, k * 2 * DV:(k + 1) * 2 * DV], start=True, stop=True)
                    full(i, L + f"kv{k}")
                operand_ready(L + "kv0", L + "kv1", L + "qT")
                for t in range(TT):
                    begin(L + f"o{t}")
                    for k in range(PAIRS):
                        for par in range(2):
                            rows = slice(DK * par, DK * par + DK)
                            for hf in range(2):
                                c = 2 * t + hf
                                i = pe.matmul(slot_banks(L + f"o{t}")[LCH * hf:LCH * hf + LCH, par, k * P:k * P + P],
                                              qT_gla[rows, k, c * LCH:c * LCH + LCH], state[rows, k, c, :], start=True, stop=True)
                    full(i, L + f"o{t}")
                pe.wait_ge(S["ymix_ready"], l + 1)
                turn(ymix, (L + "yT0", L + "yT1"))
                operand_ready(L + "yT0", L + "yT1")
                dense_rows((L + "h0", L + "h1"), 4)
                pe.wait_ge(S["mem_loaded"], 16 * (l + 1))
                turn(mem_tok, (L + "memT0", L + "memT1"))
                operand_ready(L + "memT0", L + "memT1")
                for b in range(2):
                    dense_turned(L + f"k{b}", AUX)
                dense_rows((L + "xv0", L + "xv1"), 4, AUX)
                pe.wait_ge(S["normed"], 3 * l + 1)
                turn(x, (L + "x1T0", L + "x1T1"))
                operand_ready(L + "x1T0", L + "x1T1")
                for b in range(2):
                    dense_turned(L + f"q{b}")
                operand_ready(*[L + f"{m}{b}{ab}" for m in "kq" for b in range(2) for ab in "ab"])
                for t in range(TT):
                    begin(L + f"s{t}")
                    for h in range(XH):
                        for k in range(2):
                            i = pe.matmul(slot_ps(L + f"s{t}")[:, h * T:h * T + T], qT[:, 2 * h + k, t * P:t * P + P], kT[:, 2 * h + k, :],
                                          start=(k == 0), stop=(k == 1))
                    full(i, L + f"s{t}")
                for t in range(TT):
                    begin(L + f"pT{t}")
                    pe.wait_ge(S["p_ready"], TT * l + t + 1)
                    for h in range(XH):
                        for b in range(TT):
                            i = pe.transpose(slot_ps(L + f"pT{t}")[:, (2 * h + b) * P:(2 * h + b + 1) * P], prob[:, t, h, b * P:b * P + P], ident[:])
                    full(i, L + f"pT{t}")
                operand_ready(L + "pT0", L + "pT1", L + "xv0", L + "xv1")
                for k in range(2):
                    begin(L + f"oT{k}")
                    for f in range(4):
                        fb = 4 * k + f
                        for b in range(TT):
                            i = pe.matmul(slot_ps(L + f"oT{k}")[:, f * T:f * T + T], xv[:, b, fb * P:fb * P + P], pT[:, fb // 2, b, :],
                                          start=(b == 0), stop=(b == TT - 1))
                    full(i, L + f"oT{k}")
                operand_ready(L + "oT0", L + "oT1")
                dense_rows((L + "xh0", L + "xh1"), 4)
                pe.wait_ge(S["normed"], 3 * l + 2)
                turn(x, (L + "x2T0", L + "x2T1"))
                operand_ready(L + "x2T0", L + "x2T1")
                narrow(L + "router", N_R, NE)
                experts(l)

            pe.wait_ge(S["normed"], 3 * DEPTH + 1)
            turn(h_tok, ("2.xT0", "2.xT1"))
            operand_ready("2.xT0", "2.xT1")
            dense_turned("2.q")
            dense_turned("2.k")
            dense_cols("2.v")
            for b in range(XB_BLOCKS):
                dense_turned(f"2.xb{b}")
            for name in ("z", "ga", "gb"):
                for b in range(2):
                    dense_cols(f"2.{name}{b}")
            narrow("2.dt", N_DT, SH)
            operand_ready("2.qa", "2.qb", "2.ka", "2.kb", "2.v")
            for k in range(AH // 2):
                begin(f"2.s{k}")
                for t in range(TT):
                    for par in range(2):
                        rows = slice(AD * par, AD * par + AD)
                        at = slice(0, P) if t == 0 else slice(P, P + T)
                        i = pe.matmul(slot_banks(f"2.s{k}")[:, par, at], q2T[rows, k, t * P:t * P + P], k2T[rows, k, 0:P * (t + 1)], start=True, stop=True)
                full(i, f"2.s{k}")
                begin(f"2.pT{k}")
                pe.wait_ge(S["p_ready"], TT * DEPTH + k + 1)
                pk = p2[k % 2]
                for par in range(2):
                    dst = slot_banks(f"2.pT{k}")[:, par, :]
                    pe.transpose(dst[:, 0:P], pk[:, par, 0:P], ident[:])
                    pe.transpose(dst[:, P:2 * P], pk[:, par, P:2 * P], ident[:])
                    i = pe.transpose(dst[:, 2 * P:3 * P], pk[:, par, 2 * P:3 * P], ident[:])
                full(i, f"2.pT{k}")
                begin(f"2.oT{k}")
                wait_released(pe, f"2.pT{k}")
                for par in range(2):
                    cols_h = slice((2 * k + par) * AD, (2 * k + par + 1) * AD)
                    dst = slot_banks(f"2.oT{k}")[AD * par:AD * par + AD, 0, :]
                    pe.matmul(dst[:, 0:T], v2[:, 0, cols_h], p2T[:, par, 0:T], start=True, stop=False)
                    i = pe.matmul(dst[:, P:T], v2[:, 1, cols_h], p2T[:, par, T:T + P], start=False, stop=True)
                full(i, f"2.oT{k}")
            operand_ready(*[f"2.oT{k}" for k in range(AH // 2)])
            dense_rows(("2.ya0", "2.ya1"), 2)
            begin("2.cs")
            pe.wait_ge(S["dt_ready"], 1)
            for t in range(TT):
                for b in range(t + 1):
                    i = pe.matmul(slot_ps("2.cs")[:, t * SH:t * SH + SH], tri[:, b, t * P:t * P + P], da[:, b, :], start=(b == 0), stop=(b == t))
            full(i, "2.cs")
            begin("2.csT")
            wait_released(pe, "2.cs")
            for t in range(TT):
                i = pe.transpose(slot_ps("2.csT")[0:SH, t * P:t * P + P], cs[:, t, :], ident[:])
            full(i, "2.csT")
            begin("2.cb")
            pe.wait_ge(S["xbc_ready"], XB_BLOCKS)
            for g in range(SGR):
                dst = slot_banks("2.cb")[:, g, :]
                bT, cT = xbcT[:, D // P + g, :], xbcT[:, D // P + SGR + g, :]
                pe.matmul(dst[:, 0:T], bT[:, 0:P], cT, start=True, stop=True)
                i = pe.matmul(dst[:, T:T + P], bT[:, P:T], cT[:, P:T], start=True, stop=True)
            full(i, "2.cb")
            for t in range(TT):
                begin(f"2.xs{t}")
                for b in range(D // P):
                    i = pe.transpose(slot_ps(f"2.xs{t}")[:, b * P:b * P + P], xbcT[:, b, t * P:t * P + P], ident[:])
                full(i, f"2.xs{t}")
            wait_released(pe, "2.csT")
            for k in range(SH // HB):
                begin(f"2.csb{k}")
                for h in range(HB):
                    sel = ident[0:SH, HB * k + h:HB * k + h + 1].to_broadcast([SH, P])
                    i = pe.matmul(slot_ps(f"2.csb{k}")[:, h * T:h * T + T], sel, csT[:], start=True, stop=True)
                full(i, f"2.csb{k}")
                begin(f"2.y{k}")
                pe.wait_ge(S["m_ready"], k + 1)
                operand_ready("2.xs0", "2.xs1")
                for h in range(HB):
                    hh = HB * k + h
                    for t in range(TT):
                        dst = slot_banks(f"2.y{k}")[:, t, h * SP:h * SP + SP]
                        if t == 0:
                            i = pe.matmul(dst, decay2[:, h, 0:P], xdt[:, 0, hh * SP:hh * SP + SP], start=True, stop=True)
                        else:
                            pe.matmul(dst, decay2[:, h, P:T], xdt[:, 0, hh * SP:hh * SP + SP], start=True, stop=False)
                            i = pe.matmul(dst, decay2[:, h, T:T + P], xdt[:, 1, hh * SP:hh * SP + SP], start=False, stop=True)
                full(i, f"2.y{k}")
            pe.wait_ge(S["normed"], 3 * DEPTH + 2)
            turn(zs, ("2.uT0", "2.uT1"))
            operand_ready("2.uT0", "2.uT1")
            dense_rows(("2.yb0", "2.yb1"), 4, AUX)
            pe.wait_ge(S["m2_ready"], 1)
            turn(ga, ("2.mT0", "2.mT1"))
            operand_ready("2.mT0", "2.mT1")
            dense_rows(("2.h0", "2.h1"), 4)
            pe.wait_ge(S["normed"], 3 * DEPTH + 3)
            turn(h_tok, ("2.x1T0", "2.x1T1"))
            operand_ready("2.x1T0", "2.x1T1")
            narrow("2.router", N_RE, NE + 4)
            experts(DEPTH)
            pe.wait_ge(S["p_loaded"], 16)
            turn(p_tok, ("2.pT",), PLE)
            operand_ready("2.pT")
            dense_rows(("2.pp0", "2.pp1"), 1, AUX)
            pe.wait_ge(S["moe_added"], 1)
            turn(x, ("2.x2T0", "2.x2T1"))
            operand_ready("2.x2T0", "2.x2T1")
            dense_rows(("2.pg0", "2.pg1"), 4)
            assert n == N_CHUNKS

        @block.scalar
        def _(act):
            chain = Counter(act, S["act_chain"])
            n = 0
            A = nc.scalar.activation

            def split(count):
                nonlocal n
                for _ in range(count):
                    if n < N_CHUNKS:
                        act.wait_ge(loaded[n % RAW], 16 * (n // RAW + 1))
                        if n >= SPLIT:
                            wait_used_any(act, n - SPLIT)
                        A(w_high[:, n % SPLIT, :], raw[:, n % RAW, :], ACT.Copy).then_inc(high_ready, 1)
                    n += 1

            def turned_high(dst, names, width=4):
                for k, name in enumerate(names):
                    wait_full(act, name)
                    src = slot_ps(name)[:, 0:width * T].rearrange("p (c t) -> p c t", t=T)
                    A(dst[:, width * k:width * k + width, :], src, ACT.Copy).then_inc(S["turned_high"], 1)

            def read_out(name, dst, func=ACT.Copy, scale=1.0, width=512):
                wait_full(act, name)
                frees(A(dst, slot_banks(name)[:, :, 0:width], func, scale=scale), name)

            def experts(m):
                nonlocal n
                n0, at, _ = moe_at[m]
                G, TS = ps[:, 2 * G_SLOT:2 * G_SLOT + 2, :], ps[:, 2 * T_SLOT:2 * T_SLOT + 2, :]
                with act.Fori(0, NE) as e:
                    def high(j):
                        k = n0 + j + SPLIT
                        act.wait_ge(loaded[k % RAW], 16 * e + 16 * (k // RAW + 1))
                        moe_chunk_used(act, m, e, j)
                        A(w_high[:, k % SPLIT, :], raw[:, k % RAW, :], ACT.Copy).then_inc(high_ready, 1)

                    high(0)
                    act.wait_ge(filled[G_SLOT], e + (at[G_SLOT] + 1))
                    act.wait_ge(free[U_SLOT], e + at[U_SLOT])
                    A(silu_g, G, ACT.Silu).then_inc(free[G_SLOT], 1)
                    high(1)
                    high(2)
                    high(3)
                    act.wait_ge(filled[T_SLOT], 2 * e + (at[T_SLOT] + 1))
                    A(aux_high[:, 0:FC, :], TS.rearrange("p b n -> p (b n)").rearrange("p (c t) -> p c t", t=T),
                      ACT.Copy).then_inc(S["turned_high"], 1)
                    high(4)
                    high(5)
                n = n0 + 6 * NE + SPLIT

            split(SPLIT)
            act.wait_ge(S["narrow_loaded"], 16 * (DEPTH + 4))
            A(nar_high[:], nar_raw, ACT.Copy).then_inc(S["narrow_high"], 1)
            act.wait_ge(S["small_loaded"], 96)
            act.wait_ge(S["consts_ready"], 1)
            for l in range(DEPTH):
                L = f"{l}."
                turned_high(act_high, (L + "xT0", L + "xT1"))
                for name, dst, func in (("qk", qk, ACT.Copy), ("v", v_gla, ACT.Copy), ("r", silu_r, ACT.Silu),
                                        ("u", gelu_u, ACT.Gelu_apprx_tanh), ("vs", gelu_v, ACT.Gelu_apprx_tanh)):
                    split(2)
                    read_out(L + name, dst, func)
                wait_full(act, L + "a")
                frees(A(a_tok, slot_ps(L + "a")[:, 0:TT * RANK].rearrange("p (t n) -> p t n", t=TT), ACT.Copy), L + "a")
                wait_full(act, L + "qT")
                frees(A(qT_gla, slot_ps(L + "qT")[:, 0:PAIRS * T].rearrange("p (a t) -> p a t", a=PAIRS), ACT.Copy,
                        scale=float(DK) ** -0.5), L + "qT")
                wait_full(act, L + "z")
                chain.link(A(soft, slot_ps(L + "z")[:, 0:TT * DQK].rearrange("p (t n) -> p t n", t=TT), ACT.Abs))
                chain.link(A(soft, soft, ACT.Exp, scale=-1.0))
                A(soft, soft, ACT.Ln, bias=1.0).then_inc(S["soft_ready"], 1)
                wait_full(act, L + "decay")
                A(soft, slot_banks(L + "decay")[:, 0, :].rearrange("p (t n) -> p t n", t=TT), ACT.Exp, scale=1.0 / GATE_TEMP)
                frees(A(chunk_decay, slot_banks(L + "decay")[:, 1, 0:PAIRS * NCH].rearrange("p (a c) -> p a c", a=PAIRS),
                        ACT.Exp, scale=1.0 / GATE_TEMP), L + "decay")
                for t in range(TT):
                    wait_full(act, L + f"o{t}")
                    A(osq[:, t], slot_banks(L + f"o{t}")[:, :, 0:PAIRS * P], ACT.Square).then_inc(S["osq_ready"], 1)
                turned_high(act_high, (L + "yT0", L + "yT1"))
                split(4)
                turned_high(aux_high, (L + "memT0", L + "memT1"))
                for b in range(2):
                    split(2)
                    for k, ab in enumerate("ab"):
                        f = 4 * b + 2 * k
                        read_out(L + f"k{b}{ab}", kT[:, f:f + 2, :], width=T)
                split(4)
                for t in range(TT):
                    read_out(L + f"xv{t}", xv[:, t, :].rearrange("p (b n) -> p b n", b=2))
                turned_high(act_high, (L + "x1T0", L + "x1T1"))
                for b in range(2):
                    split(2)
                    for k, ab in enumerate("ab"):
                        f = 4 * b + 2 * k
                        read_out(L + f"q{b}{ab}", qT[:, f:f + 2, :], width=T)
                for t in range(TT):
                    act.wait_ge(S["smax_ready"], TT * l + t + 1)
                    for h in range(XH):
                        i = A(prob[:, t, h, :], slot_ps(L + f"s{t}")[:, h * T:h * T + T], ACT.Exp, bias=neg_max[:, t, h:h + 1],
                              scale=float(XD) ** -0.5, accum_out=p_sum[:, t, h:h + 1])
                    frees(i, L + f"s{t}")
                for t in range(TT):
                    wait_full(act, L + f"pT{t}")
                    frees(A(pT[:, :, :, t * P:t * P + P], slot_ps(L + f"pT{t}").rearrange("p (h b t) -> p h b t", h=XH, b=TT),
                            ACT.Copy), L + f"pT{t}")
                turned_high(act_high, (L + "oT0", L + "oT1"))
                split(4)
                turned_high(act_high, (L + "x2T0", L + "x2T1"))
                act.wait_ge(S["router_max"], l + 1)
                A(probs, probs, ACT.Exp).then_inc(S["router_exp"], 1)
                experts(l)

            turned_high(act_high, ("2.xT0", "2.xT1"))
            for name, dst, scale in (("q", q2T, float(AD) ** -0.5), ("k", k2T, 1.0)):
                split(2)
                for k, ab in enumerate("ab"):
                    read_out(f"2.{name}{ab}", dst[:, 2 * k:2 * k + 2, :], scale=scale, width=T)
            split(2)
            read_out("2.v", v2)

            def conv_silu(b):
                act.wait_ge(S["conv_done"], b + 1)
                for f in range(4):
                    c = 4 * b + f
                    i = A(xbcT[:, c, :], xbcT[:, c, :], ACT.Silu, bias=conv_b[:, c:c + 1])
                i.then_inc(S["xbc_ready"], 1)

            for b in range(XB_BLOCKS):
                split(2)
                if b >= 2:
                    act.wait_ge(S["conv_done"], b - 1)
                elif b == 0:
                    act.wait_ge(S["normed"], 3 * DEPTH + 1)
                for k, ab in enumerate("ab"):
                    read_out(f"2.xb{b}{ab}", pad[b % 2][:, 2 * k:2 * k + 2, CONV - 1:PADW], width=T)
                if b:
                    conv_silu(b - 1)
            for b in range(2):
                split(2)
                read_out(f"2.z{b}", zs[:, :, 512 * b:512 * b + 512], ACT.Silu)
                if b == 0:
                    conv_silu(XB_BLOCKS - 1)
            for name, dst in (("ga", ga), ("gb", gb)):
                for b in range(2):
                    split(2)
                    read_out(f"2.{name}{b}", dst[:, :, 512 * b:512 * b + 512], ACT.Sigmoid)
            wait_released(act, "2.dt")
            chain.link(A(dt_soft, dt_in, ACT.Abs))
            chain.link(A(dt_soft, dt_soft, ACT.Exp, scale=-1.0))
            A(neg_a, neg_a, ACT.Exp)
            A(dt_soft, dt_soft, ACT.Ln, bias=1.0).then_inc(S["dt_soft"], 1)
            for k in range(AH // 2):
                act.wait_ge(S["smax_ready"], TT * DEPTH + k + 1)
                pk = p2[k % 2]
                for t, at in enumerate((slice(0, P), slice(P, P + T))):
                    for par in range(2):
                        i = A(pk[:, par, at], pk[:, par, at], ACT.Exp, bias=neg_max2[:, t, par:par + 1], accum_out=p_sum2[:, t, par:par + 1])
                i.then_inc(S["exp_ready"], 1)
                read_out(f"2.pT{k}", p2T, width=P + T)
                turned_high(act_high[:, k:k + 1, :], (f"2.oT{k}",), 1)
            split(2)
            for k in range(SH // HB):
                wait_released(act, f"2.csb{k}")
                A(decay2, decay2, ACT.Exp).then_inc(S["e_ready"], 1)
            act.wait_ge(S["u_ready"], 1)
            for t in range(TT):
                for g in range(SGR):
                    i = A(usq[:, t, g * 512:g * 512 + 512], zs[:, t, g * 512:g * 512 + 512], ACT.Square, accum_out=u_ms[:, t, g:g + 1])
            i.then_inc(S["usq_ready"], 1)
            turned_high(aux_high, ("2.uT0", "2.uT1"))
            split(4)
            turned_high(act_high, ("2.mT0", "2.mT1"))
            split(4)
            turned_high(act_high, ("2.x1T0", "2.x1T1"))
            act.wait_ge(S["router_max"], DEPTH + 1)
            A(g_prob, g_prob, ACT.Exp).then_inc(S["router_exp"], 1)
            act.wait_ge(S["arg_ready"], 1)
            A(probs, probs, ACT.Exp).then_inc(S["arg_exp"], 1)
            experts(DEPTH)
            turned_high(aux_high, ("2.pT",), PLE // P)
            split(1)
            for t in range(TT):
                read_out(f"2.pp{t}", pp[:, t, :].rearrange("p (b n) -> p b n", b=2))
            turned_high(act_high, ("2.x2T0", "2.x2T1"))
            split(4)
            for t in range(TT):
                read_out(f"2.pg{t}", sig[:, t, :].rearrange("p (b n) -> p b n", b=2), ACT.Sigmoid)

        @block.vector
        def _(dve):
            V = nc.vector
            chain = Counter(dve, S["dve_chain"])
            link = chain.link
            n = 0
            turned = 0

            def split(count):
                nonlocal n
                for _ in range(count):
                    if n < N_CHUNKS:
                        dve.wait_ge(high_ready, n + 1)
                        V.tensor_tensor(w_low[:, n % SPLIT, :], raw[:, n % RAW, :], w_high[:, n % SPLIT, :].bitcast(F32),
                                        ALU.subtract).then_inc(low_ready, 1)
                    n += 1

            def turned_low(low, high, names, width=4):
                nonlocal turned
                for k, name in enumerate(names):
                    turned += 1
                    dve.wait_ge(S["turned_high"], turned)
                    src = slot_ps(name)[:, 0:width * T].rearrange("p (c t) -> p c t", t=T)
                    frees(V.tensor_tensor(low[:, width * k:width * k + width, :], src,
                                          high[:, width * k:width * k + width, :].bitcast(F32), ALU.subtract), name)

            def rsqrt(at, count):
                v = st[:, at:at + count]
                y, h, q = (st[:, 640 + 8 * k:640 + 8 * k + count] for k in range(3))
                yi = y.bitcast(mybir.dt.int32)
                link(V.tensor_scalar(yi, v.bitcast(mybir.dt.int32), 1, None, ALU.logical_shift_right))
                link(V.tensor_scalar(yi, yi, -1.0, float(0x5F3759DF), ALU.mult, ALU.add))
                link(V.tensor_scalar(h, v, -0.5, None, ALU.mult))
                for k in range(4):
                    link(V.tensor_tensor(q, y, y, ALU.mult))
                    link(V.tensor_tensor(q, q, h, ALU.mult))
                    link(V.scalar_tensor_tensor(v if k == 3 else y, q, 1.5, y, ALU.add, ALU.mult))

            def layer_norm(k, src):
                for t in range(TT):
                    for b in range(2):
                        i = V.bn_stats(bn[:, t, b, :], src[:, t, 512 * b:512 * b + 512])
                link(i)
                for t in range(TT):
                    i = V.bn_aggr(mean_var[:, t, :], bn[:, t, :, :])
                link(i)
                link(V.tensor_scalar(rstd, mean_var[:, :, 1:2], LN_EPS, None, ALU.add))
                rsqrt(28, TT)
                dve.wait_ge(S["norm_loaded"], 16 * 0 + norm_need[k])
                for t in range(TT):
                    i = V.scalar_tensor_tensor(src[:, t, :], src[:, t, :], mean_var[:, t, 0:1], norm_p[:, 0, :], ALU.subtract, ALU.mult)
                link(i)
                for t in range(TT):
                    i = V.scalar_tensor_tensor(x[:, t, :], src[:, t, :], rstd[:, t, :], norm_p[:, 1, :], ALU.mult, ALU.add)
                i.then_inc(S["normed"], 1)

            def rms_norm(k, src, dst, scratch):
                for t in range(TT):
                    i = V.scalar_tensor_tensor(scratch[:, t, :], src[:, t, :], 1.0, src[:, t, :], ALU.mult, ALU.mult, accum_out=rstd[:, t, :])
                link(i)
                link(V.tensor_scalar(rstd, rstd, 1.0 / D, RMS_EPS, ALU.mult, ALU.add))
                rsqrt(28, TT)
                dve.wait_ge(S["norm_loaded"], norm_need[k])
                for t in range(TT):
                    i = V.scalar_tensor_tensor(dst[:, t, :], src[:, t, :], rstd[:, t, :], norm_p[:, 0, :], ALU.mult, ALU.mult)
                i.then_inc(S["normed"], 1)

            def add_branch(names, dst, scale):
                for t, name in enumerate(names):
                    wait_full(dve, name)
                    i = V.scalar_tensor_tensor(dst[:, t, :], x[:, t, :], scale, slot_ps(name), ALU.mult, ALU.add)
                    frees(i, name)
                    wait_released(dve, name)

            def ranks(v):
                link(V.tensor_tensor(rank[:, :, :, 1:4], v[:, :, :, 0:1].to_broadcast([P, TT, 4, 3]), v[:, :, :, 1:4], ALU.is_ge))
                link(V.tensor_tensor(rank[:, :, :, 0:1], v[:, :, :, 1:2], v[:, :, :, 0:1], ALU.is_gt))
                for j in range(1, 4):
                    if j > 1:
                        link(V.tensor_tensor(beat[:, :, :, 0:j], v[:, :, :, j:j + 1].to_broadcast([P, TT, 4, j]), v[:, :, :, 0:j], ALU.is_gt))
                        link(V.tensor_tensor(rank[:, :, :, 0:j], rank[:, :, :, 0:j], beat[:, :, :, 0:j], ALU.add))
                    if j < 3:
                        link(V.tensor_tensor(beat[:, :, :, j + 1:4], v[:, :, :, j:j + 1].to_broadcast([P, TT, 4, 3 - j]), v[:, :, :, j + 1:4], ALU.is_ge))
                        link(V.tensor_tensor(rank[:, :, :, j + 1:4], rank[:, :, :, j + 1:4], beat[:, :, :, j + 1:4], ALU.add))

            def first_best(score):
                link(V.tensor_reduce(g_max, score, AX, ALU.max))
                link(V.tensor_tensor(g_eq, score, g_max.to_broadcast([P, TT, 4]), ALU.is_ge))
                for g in range(1, 4):
                    link(V.tensor_tensor(g_seen[:, :, g:g + 1], g_seen[:, :, g - 1:g], g_eq[:, :, g - 1:g], ALU.max))
                link(V.tensor_tensor(g_first, g_eq, g_seen, ALU.is_gt))

            def normalised(weight):
                link(V.tensor_reduce(r_sum, weight, AX, ALU.add))
                link(V.reciprocal(r_inv, r_sum))

            groups = lambda v: v.rearrange("p t (g e) -> p t g e", g=4)
            over_e = lambda v: v.unsqueeze(3).to_broadcast([P, TT, 4, 4])
            flat = lambda v: v.rearrange("p t g e -> p t (g e)")

            def route_one(l):
                name = f"{l}.router"
                wait_full(dve, name)
                src = slot_ps(name)[:, 0:TT * NE].rearrange("p (t n) -> p t n", t=TT)
                frees(V.tensor_tensor(logits[:, :, 0:NE], src, b_router.unsqueeze(1).to_broadcast([P, TT, NE]), ALU.add), name)
                wait_released(dve, name)
                link(V.tensor_reduce(r_max, logits[:, :, 0:NE], AX, ALU.max))
                V.tensor_tensor(probs, logits[:, :, 0:NE], r_max.to_broadcast([P, TT, NE]), ALU.subtract).then_inc(S["router_max"], 1)
                dve.wait_ge(S["router_exp"], l + 1)
                normalised(probs)
                link(V.tensor_tensor(probs, probs, r_inv.to_broadcast([P, TT, NE]), ALU.mult))
                ranks(groups(probs))
                link(V.scalar_tensor_tensor(flat(top), flat(rank), 2.0, probs, ALU.is_lt, ALU.mult))
                link(V.tensor_reduce(g_score, top, AX, ALU.add))
                first_best(g_score)
                link(V.tensor_tensor(top, top, over_e(g_first), ALU.mult))
                normalised(flat(top))
                link(V.tensor_tensor(gates, flat(top), r_inv.to_broadcast([P, TT, NE]), ALU.mult))

            def route_two():
                name = "2.router"
                wait_full(dve, name)
                src = slot_ps(name)[:, 0:TT * (NE + 4)].rearrange("p (t n) -> p t n", t=TT)
                frees(V.tensor_tensor(logits, src, b_re.unsqueeze(1).to_broadcast([P, TT, NE + 4]), ALU.add), name)
                wait_released(dve, name)
                link(V.tensor_reduce(r_max, logits[:, :, NE:NE + 4], AX, ALU.max))
                V.tensor_tensor(g_prob, logits[:, :, NE:NE + 4], r_max.to_broadcast([P, TT, 4]), ALU.subtract).then_inc(S["router_max"], 1)
                dve.wait_ge(S["router_exp"], DEPTH + 1)
                normalised(g_prob)
                link(V.tensor_tensor(g_prob, g_prob, r_inv.to_broadcast([P, TT, 4]), ALU.mult))
                first_best(g_prob)
                ev = groups(logits[:, :, 0:NE])
                ranks(ev)
                link(V.tensor_scalar(top, rank, 2.0, None, ALU.is_lt))
                link(V.tensor_tensor(top, top, over_e(g_first), ALU.mult))
                link(V.tensor_reduce(e_max, ev, AX, ALU.max))
                link(V.tensor_tensor(e_pick, e_max, g_first, ALU.mult))
                link(V.tensor_reduce(m_sel, e_pick, AX, ALU.add))
                link(V.tensor_tensor(probs, logits[:, :, 0:NE], m_sel.to_broadcast([P, TT, NE]), ALU.subtract))
                V.tensor_tensor(probs, probs, flat(top), ALU.mult).then_inc(S["arg_ready"], 1)
                dve.wait_ge(S["arg_exp"], 1)
                link(V.tensor_tensor(probs, probs, flat(top), ALU.mult))
                normalised(probs)
                link(V.tensor_tensor(r_inv, r_inv, g_max, ALU.mult))
                link(V.tensor_tensor(gates, probs, r_inv.to_broadcast([P, TT, NE]), ALU.mult))

            def experts(m):
                nonlocal n, turned
                n0, at, _ = moe_at[m]
                U, TS, Y0 = (ps[:, 2 * s:2 * s + 2, :] for s in (U_SLOT, T_SLOT, Y0_SLOT))
                flat2 = lambda b: b.rearrange("p b n -> p (b n)")
                with dve.Fori(0, NE) as e:
                    def low(j):
                        k = n0 + j + SPLIT
                        dve.wait_ge(high_ready, 6 * e + (k + 1))
                        V.tensor_tensor(w_low[:, k % SPLIT, :], raw[:, k % RAW, :], w_high[:, k % SPLIT, :].bitcast(F32),
                                        ALU.subtract).then_inc(low_ready, 1)

                    low(0)
                    low(1)
                    low(2)
                    dve.wait_ge(filled[U_SLOT], e + (at[U_SLOT] + 1))
                    dve.wait_ge(free[G_SLOT], e + (at[G_SLOT] + 1))
                    for t in range(TT):
                        i = V.scalar_tensor_tensor(hid[:, t, :], silu_g[:, t, :], gates[:, t, bass.ds(e, 1)], U[:, t, :], ALU.mult, ALU.mult)
                    i.then_inc(free[U_SLOT], 1)
                    low(3)
                    dve.wait_ge(S["turned_high"], e + (turned + 1))
                    V.tensor_tensor(aux_low[:, 0:FC, :], flat2(TS).rearrange("p (c t) -> p c t", t=T),
                                    aux_high[:, 0:FC, :].bitcast(F32), ALU.subtract).then_inc(free[T_SLOT], 1)
                    low(4)
                    low(5)
                    dve.wait_ge(filled[Y0_SLOT], e + (at[Y0_SLOT] + 1))
                    V.tensor_tensor(y_acc[:, 0, :], y_acc[:, 0, :], flat2(Y0), ALU.add).then_inc(free[Y0_SLOT], 1)
                    dve.wait_ge(filled[T_SLOT], 2 * e + (at[T_SLOT] + 2))
                    V.tensor_tensor(y_acc[:, 1, :], y_acc[:, 1, :], flat2(TS), ALU.add).then_inc(free[T_SLOT], 1)
                n = n0 + 6 * NE + SPLIT
                turned += NE
                dve.wait_ge(free[T_SLOT], at[T_SLOT] + 2 * NE)

            split(SPLIT)
            dve.wait_ge(S["narrow_high"], 1)
            V.tensor_tensor(nar_low[:], nar_raw, nar_high[:].bitcast(F32), ALU.subtract).then_inc(S["narrow_ready"], 1)
            dve.wait_ge(S["consts_ready"], 1)
            dve.wait_ge(S["small_loaded"], 96)
            wait_full(dve, "colc")
            frees(V.tensor_copy(colc[:], slot_ps("colc")[:, 0:colc.shape[1]]), "colc")
            wait_released(dve, "colc")
            for l in range(DEPTH):
                L = f"{l}."
                turned_low(act_low, act_high, (L + "xT0", L + "xT1"))
                link(V.memset(aT, 1.0))
                split(10)
                wait_released(dve, L + "vs")
                for t in range(TT):
                    for g in range(SG):
                        i = V.bn_stats(v_bn[:, t, g, :], gelu_v[:, t, g * P:g * P + P])
                link(i)
                for t in range(TT):
                    for g in range(SG):
                        i = V.bn_aggr(v_mv[:, t, g, :], v_bn[:, t, g, :])
                link(i)
                link(V.tensor_scalar(v_rstd, v_mv[:, :, :, 1:2], LN_EPS, None, ALU.add))
                rsqrt(128, TT * SG)
                dve.wait_ge(S["mixp_loaded"], 96 * (l + 1))
                for t in range(TT):
                    for g in range(SG):
                        at = slice(g * P, g * P + P)
                        i = V.scalar_tensor_tensor(gelu_v[:, t, at], gelu_v[:, t, at], v_mv[:, t, g, 0:1], sln_g[:, at], ALU.subtract, ALU.mult)
                link(i)
                for t in range(TT):
                    for g in range(SG):
                        at = slice(g * P, g * P + P)
                        i = V.scalar_tensor_tensor(gelu_v[:, t, at], gelu_v[:, t, at], v_rstd[:, t, g, :], sln_b[:, at], ALU.mult, ALU.add)
                i.then_inc(S["vnorm_ready"], 1)
                wait_full(dve, L + "wsT")
                link(V.tensor_copy(wsT, slot_ps(L + "wsT")[:, 0:SG * P].rearrange("p (g t) -> p g t", g=SG)))
                frees(V.memset(wsT[LCH:P, :, 0:LCH], 0.0), L + "wsT")
                wait_full(dve, L + "aT")
                frees(V.tensor_copy(aT[0:RANK], slot_ps(L + "aT")[0:RANK, 0:T]), L + "aT")
                wait_full(dve, L + "z")
                z = slot_ps(L + "z")[:, 0:TT * DQK].rearrange("p (t n) -> p t n", t=TT)
                dve.wait_ge(S["soft_ready"], l + 1)
                frees(V.scalar_tensor_tensor(log_a, z, 0.0, soft, ALU.min, ALU.subtract), L + "z")
                wait_full(dve, L + "mix_sgu")
                for t in range(TT):
                    for g in range(SG):
                        at = slice(g * P, g * P + P)
                        i = V.scalar_tensor_tensor(ymix[:, t, DGLA + g * P:DGLA + g * P + P], slot_banks(L + "mix_sgu")[:, t, at],
                                                   b_s[l][:, g:g + 1], gelu_u[:, t, at], ALU.add, ALU.mult)
                frees(i, L + "mix_sgu")
                wait_released(dve, L + "decay")
                V.tensor_tensor(k_dec, qk[:, :, DQK:2 * DQK], soft, ALU.mult).then_inc(S["kdec_ready"], 1)
                for k in range(PAIRS):
                    wait_full(dve, L + f"kv{k}")
                    for c in range(NCH):
                        t, hf = c // 2, c % 2
                        for par in range(2):
                            rows = slice(DK * par, DK * par + DK)
                            kv = slot_banks(L + f"kv{k}")[rows, hf, 2 * DV * t + DV * par:2 * DV * t + DV * par + DV]
                            if c == 0:
                                i = V.tensor_copy(state[rows, k, c, :], kv)
                            else:
                                i = V.scalar_tensor_tensor(state[rows, k, c, :], state[rows, k, c - 1, :], chunk_decay[rows, k, c:c + 1],
                                                           kv, ALU.mult, ALU.add)
                        if c < NCH - 1:
                            link(i)
                    frees(i, L + f"kv{k}")
                dve.wait_ge(S["srg_ready"], TT * (l + 1))
                for t in range(TT):
                    dve.wait_ge(S["osq_ready"], TT * l + t + 1)
                    link(V.tensor_reduce(o_ms[:, t, :], osq[:, t].rearrange("p b (a n) -> p b a n", a=PAIRS), AX, ALU.add))
                    link(V.tensor_scalar(o_rs[:, t, :], o_ms[:, t, :], 1.0 / DV, RMS_EPS, ALU.mult, ALU.add))
                    rsqrt(48 + GH * t, GH)
                    for par in range(2):
                        for k in range(PAIRS):
                            at = slice((2 * k + par) * DV, (2 * k + par + 1) * DV)
                            i = V.scalar_tensor_tensor(ymix[:, t, at], slot_banks(L + f"o{t}")[:, par, k * P:k * P + P],
                                                       o_rs[:, t, PAIRS * par + k:PAIRS * par + k + 1], silu_r[:, t, at], ALU.mult, ALU.mult)
                    frees(i, L + f"o{t}")
                dve.wait_ge(free[job[L + "o1"][0]], job[L + "o1"][1] + 1)
                V.tensor_copy(o_ms[:, 0, 0:1], o_rs[:, 0, 0:1]).then_inc(S["ymix_ready"], 1)
                turned_low(act_low, act_high, (L + "yT0", L + "yT1"))
                split(4)
                add_branch((L + "h0", L + "h1"), summed, ALPHA)
                layer_norm(3 * l, summed)
                turned_low(aux_low, aux_high, (L + "memT0", L + "memT1"))
                split(8)
                turned_low(act_low, act_high, (L + "x1T0", L + "x1T1"))
                split(4)
                for t in range(TT):
                    wait_full(dve, L + f"s{t}")
                    link(V.tensor_reduce(neg_max[:, t, :], slot_ps(L + f"s{t}").rearrange("p (h m) -> p h m", h=XH), AX, ALU.max))
                    V.tensor_scalar(neg_max[:, t, :], neg_max[:, t, :], -(float(XD) ** -0.5), None, ALU.mult).then_inc(S["smax_ready"], 1)
                for t in range(TT):
                    wait_released(dve, L + f"s{t}")
                    link(V.reciprocal(p_inv[:, t, :], p_sum[:, t, :]))
                    for h in range(XH):
                        i = V.tensor_scalar(prob[:, t, h, :], prob[:, t, h, :], p_inv[:, t, h:h + 1], None, ALU.mult)
                    i.then_inc(S["p_ready"], 1)
                turned_low(act_low, act_high, (L + "oT0", L + "oT1"))
                split(4)
                add_branch((L + "xh0", L + "xh1"), summed, ALPHA)
                layer_norm(3 * l + 1, summed)
                turned_low(act_low, act_high, (L + "x2T0", L + "x2T1"))
                route_one(l)
                link(V.tensor_scalar(y_acc, x[:], ALPHA, None, ALU.mult))
                experts(l)
                layer_norm(3 * l + 2, y_acc)

            for k in range(2):
                link(V.memset(pad[k][:, :, 0:CONV - 1], 0.0))
            dve.wait_ge(S["normed"], 3 * DEPTH)
            rms_norm(3 * DEPTH, x, h_tok, W3[:].rearrange("p (t n) -> p t n", t=TT))
            turned_low(act_low, act_high, ("2.xT0", "2.xT1"))
            split(6)
            for b in range(XB_BLOCKS):
                split(2)
                for ab in "ab":
                    wait_released(dve, f"2.xb{b}{ab}")
                for k in range(CONV):
                    for f in range(4):
                        c = 4 * b + f
                        src = pad[b % 2][:, f, k:k + T]
                        if k == 0:
                            i = V.tensor_scalar(xbcT[:, c, :], src, conv_w[0][:, c:c + 1], None, ALU.mult)
                        else:
                            i = V.scalar_tensor_tensor(xbcT[:, c, :], src, conv_w[k][:, c:c + 1], xbcT[:, c, :], ALU.mult, ALU.add)
                    if k < CONV - 1:
                        link(i)
                i.then_inc(S["conv_done"], 1)
            split(12)
            wait_full(dve, "2.dt")
            frees(V.tensor_tensor(dt_in, slot_ps("2.dt")[:, 0:TT * SH].rearrange("p (t n) -> p t n", t=TT),
                                  dt_bias.unsqueeze(1).to_broadcast([P, TT, SH]), ALU.add), "2.dt")
            wait_released(dve, "2.dt")
            dve.wait_ge(S["dt_soft"], 1)
            link(V.scalar_tensor_tensor(dt, dt_in, 0.0, dt_soft, ALU.max, ALU.add))
            V.scalar_tensor_tensor(da, dt, -1.0, neg_a.unsqueeze(1).to_broadcast([P, TT, SH]), ALU.mult, ALU.mult).then_inc(S["dt_ready"], 1)
            spans = (slice(0, P), slice(P, P + T))
            for k in range(AH // 2):
                pk = p2[k % 2]
                wait_full(dve, f"2.s{k}")
                for par in range(2):
                    slope = 2.0 ** (-8.0 * (2 * k + par + 1) / AH)
                    i = V.scalar_tensor_tensor(pk[:, par, :], dist[:], slope, slot_banks(f"2.s{k}")[:, par, 0:P + T], ALU.mult, ALU.add)
                frees(i, f"2.s{k}")
                wait_released(dve, f"2.s{k}")
                for t in range(TT):
                    i = V.tensor_reduce(neg_max2[:, t, :], pk[:, :, spans[t]], AX, ALU.max)
                link(i)
                V.tensor_scalar(neg_max2, neg_max2, -1.0, None, ALU.mult).then_inc(S["smax_ready"], 1)
                dve.wait_ge(S["exp_ready"], k + 1)
                link(V.reciprocal(p_inv2, p_sum2))
                for t in range(TT):
                    for par in range(2):
                        i = V.tensor_scalar(pk[:, par, spans[t]], pk[:, par, spans[t]], p_inv2[:, t, par:par + 1], None, ALU.mult)
                i.then_inc(S["p_ready"], 1)
                turned_low(act_low[:, k:k + 1, :], act_high[:, k:k + 1, :], (f"2.oT{k}",), 1)
            split(2)
            for t in range(TT):
                wait_full(dve, f"2.ya{t}")
                if t == 0:
                    wait_released(dve, "2.ga1")
                frees(V.tensor_tensor(ga[:, t, :], ga[:, t, :], slot_ps(f"2.ya{t}"), ALU.mult), f"2.ya{t}")
            wait_full(dve, "2.cs")
            frees(V.tensor_copy(cs, slot_ps("2.cs")[:, 0:TT * SH].rearrange("p (t n) -> p t n", t=TT)), "2.cs")
            wait_full(dve, "2.csT")
            frees(V.tensor_copy(csT[:], slot_ps("2.csT")[0:SH, 0:T]), "2.csT")
            heads = lambda v: v.rearrange("p (h n) -> p h n", h=SH)
            for t in range(TT):
                wait_full(dve, f"2.xs{t}")
                src = heads(slot_ps(f"2.xs{t}"))
                V.tensor_tensor(heads(xdt[:, t, :]), src, dt[:, t, :].unsqueeze(2).to_broadcast([P, SH, SP]), ALU.mult)
                frees(V.tensor_tensor(heads(xs[:, t, :]), src, d_skip.unsqueeze(2).to_broadcast([P, SH, SP]), ALU.mult), f"2.xs{t}")
            wait_full(dve, "2.cb")
            for g in range(SGR):
                V.tensor_tensor(cbT[:, g, 0:T], slot_banks("2.cb")[:, g, 0:T], tri[:, 0, :], ALU.mult)
                i = V.tensor_tensor(cbT[:, g, T:T + P], slot_banks("2.cb")[:, g, T:T + P], tri[:, 1, P:T], ALU.mult)
            frees(i, "2.cb")
            wait_released(dve, "2.cb")
            zeroed = None
            for k in range(SH // HB):
                wait_full(dve, f"2.csb{k}")
                for h in range(HB):
                    hh = HB * k + h
                    src = slot_ps(f"2.csb{k}")[:, h * T:h * T + T]
                    V.tensor_scalar(decay2[:, h, 0:T], src, cs[:, 0, hh:hh + 1], 0.0, ALU.subtract, ALU.min)
                    i = V.tensor_scalar(decay2[:, h, T:T + P], src[:, P:T], cs[:, 1, hh:hh + 1], 0.0, ALU.subtract, ALU.min)
                frees(i, f"2.csb{k}")
                dve.wait_ge(S["e_ready"], k + 1)
                g = HB * k // (SH // SGR)
                V.tensor_tensor(decay2, decay2, cbT[:, g, :].unsqueeze(1).to_broadcast([P, HB, T + P]), ALU.mult).then_inc(S["m_ready"], 1)
                wait_full(dve, f"2.y{k}")
                at = slice(HB * SP * k, HB * SP * (k + 1))
                frees(V.tensor_tensor(xs[:, :, at], xs[:, :, at], slot_banks(f"2.y{k}")[:, :, 0:HB * SP], ALU.add), f"2.y{k}")
            wait_released(dve, f"2.y{SH // HB - 1}")
            wait_released(dve, "2.z1")
            V.tensor_tensor(zs, zs, xs, ALU.mult).then_inc(S["u_ready"], 1)
            dve.wait_ge(S["usq_ready"], 1)
            link(V.tensor_scalar(u_rs, u_ms, float(SGR) / D, RMS_EPS, ALU.mult, ALU.add))
            rsqrt(624, TT * SGR)
            dve.wait_ge(S["norm_loaded"], norm_need[3 * DEPTH + 1])
            for t in range(TT):
                for g in range(SGR):
                    at = slice(g * 512, g * 512 + 512)
                    i = V.scalar_tensor_tensor(zs[:, t, at], zs[:, t, at], u_rs[:, t, g:g + 1], norm_p[:, 0, at], ALU.mult, ALU.mult)
            i.then_inc(S["normed"], 1)
            turned_low(aux_low, aux_high, ("2.uT0", "2.uT1"))
            split(4)
            for t in range(TT):
                wait_full(dve, f"2.yb{t}")
                if t == 0:
                    wait_released(dve, "2.gb1")
                frees(V.tensor_tensor(gb[:, t, :], gb[:, t, :], slot_ps(f"2.yb{t}"), ALU.mult), f"2.yb{t}")
            wait_released(dve, "2.yb1")
            V.tensor_tensor(ga, ga, gb, ALU.add).then_inc(S["m2_ready"], 1)
            turned_low(act_low, act_high, ("2.mT0", "2.mT1"))
            split(4)
            add_branch(("2.h0", "2.h1"), x, 1.0)
            rms_norm(3 * DEPTH + 2, x, h_tok, W2[:].rearrange("p (t n) -> p t n", t=TT))
            turned_low(act_low, act_high, ("2.x1T0", "2.x1T1"))
            route_two()
            link(V.tensor_copy(y_acc, x[:]))
            experts(DEPTH)
            V.tensor_copy(x[:], y_acc).then_inc(S["moe_added"], 1)
            turned_low(aux_low, aux_high, ("2.pT",), PLE // P)
            split(1)
            turned_low(act_low, act_high, ("2.x2T0", "2.x2T1"))
            split(4)
            for t in range(TT):
                wait_released(dve, f"2.pp{t}")
                wait_released(dve, f"2.pg{t}")
                i = V.tensor_tensor(sig[:, t, :], sig[:, t, :], pp[:, t, :], ALU.mult)
            link(i)
            link(V.tensor_tensor(x[:], x[:], sig, ALU.add))
            rms_norm(3 * DEPTH + 3, x, sig, pp)


def kernel(**inputs):
    import numpy as np
    import concourse.bacc as bacc
    from concourse.bass_utils import run_bass_kernel_spmd

    nc = bacc.Bacc("TRN2", target_bir_lowering=False, num_devices=1)
    arrays, args = {}, {}
    for name, value in inputs.items():
        value = np.ascontiguousarray(value)
        arrays[f"in_{name}"] = value
        args[name] = nc.dram_tensor(f"in_{name}", value.shape, mybir.dt.from_np(value.dtype), kind="ExternalInput").ap()
    shape = inputs["x"].shape
    out = nc.dram_tensor("out", shape, F32, kind="ExternalOutput").ap()
    build(nc, args, out)
    return run_bass_kernel_spmd(nc, [arrays], core_ids=[0]).results[0]["out"]
```
